# Optimizing a Trainium2 kernel written in Bass

```python
import math
import jax, jax.numpy as jnp
from jax import lax
import numpy as np

D_MODEL = 1024
BATCH = 1
SEQ = 2048
DEPTH = 2

CHUNK = 64
Q_BLOCK = 128
ROPE_THETA = 10000.0
EPS = 1e-6

DIFF_HEADS = 4
DIFF_HEAD_DIM = 64
DIFF_V_DIM = 2 * DIFF_HEAD_DIM
DIFF_QK = DIFF_HEADS * 2 * DIFF_HEAD_DIM
DIFF_WIDTH = DIFF_HEADS * DIFF_V_DIM
POOL_WINDOWS = (2, 4, 8, 16)
POOL_GROUPS = len(POOL_WINDOWS)
POOL_WIDTH = D_MODEL // 2
POOL_GROUP_DIM = POOL_WIDTH // POOL_GROUPS
AB_WIDTH = DIFF_WIDTH + POOL_WIDTH
AB_IN = 2 * DIFF_QK + DIFF_WIDTH + POOL_WIDTH + AB_WIDTH

SWA_HEADS = 16
SWA_KV_HEADS = 2
SWA_GROUP = SWA_HEADS // SWA_KV_HEADS
SWA_HEAD_DIM = 64
SWA_WIDTH = SWA_HEADS * SWA_HEAD_DIM
SWA_KV = SWA_KV_HEADS * SWA_HEAD_DIM
SWA_WINDOW = 128
WINDOW_CHUNKS = SWA_WINDOW // CHUNK
C_IN = SWA_WIDTH + 2 * SWA_KV + SWA_WIDTH

N_EVEN = (DEPTH + 1) // 2
N_ODD = DEPTH // 2

kernel_name = "hybrid_diffattn_pool_swa_sandwich"

def rmsnorm(x, g):
    xf = x.astype(jnp.float32)
    y = xf * lax.rsqrt(jnp.mean(xf * xf, axis=-1, keepdims=True) + EPS)
    return (y * g.astype(jnp.float32)).astype(x.dtype)

def rope_tables(length, dim):
    inv_freq = ROPE_THETA ** (-jnp.arange(0, dim, 2, dtype=jnp.float32) / dim)
    pos = jnp.arange(length, dtype=jnp.float32)
    ang = pos[:, None] * inv_freq[None, :]
    ang = jnp.concatenate([ang, ang], axis=-1)
    return jnp.cos(ang), jnp.sin(ang)

def apply_rope(x, cos, sin):
    extra = x.ndim - 3
    c = cos.reshape(cos.shape[0], *([1] * extra), cos.shape[1])
    s = sin.reshape(sin.shape[0], *([1] * extra), sin.shape[1])
    xf = x.astype(jnp.float32)
    x1, x2 = jnp.split(xf, 2, axis=-1)
    rot = jnp.concatenate([-x2, x1], axis=-1)
    return (xf * c + rot * s).astype(x.dtype)

def diff_attention(q, k, v, lam):
    B, L, H, _, Dh = q.shape
    nb = L // Q_BLOCK
    scale = Dh ** -0.5
    qb = jnp.moveaxis(q.reshape(B, nb, Q_BLOCK, H, 2, Dh), 1, 0)
    key_chunk = jnp.arange(L) // CHUNK

    def block(args):
        qi, i = args
        s = jnp.einsum('bqhcd,bkhcd->bhcqk', qi, k).astype(jnp.float32) * scale
        q_chunk = (i * Q_BLOCK + jnp.arange(Q_BLOCK)) // CHUNK
        mask = key_chunk[None, :] <= q_chunk[:, None]
        s = jnp.where(mask[None, None, None], s, -jnp.inf)
        p = jax.nn.softmax(s, axis=-1)
        a = p[:, :, 0] - lam * p[:, :, 1]
        return jnp.einsum('bhqk,bkhd->bqhd', a.astype(v.dtype), v)

    o = lax.map(block, (qb, jnp.arange(nb)))
    return jnp.moveaxis(o, 0, 1).reshape(B, L, H, v.shape[-1])

def multiscale_pool(u, w, scale):
    B, L, _ = u.shape
    ug = u.reshape(B, L, POOL_GROUPS, POOL_GROUP_DIM)
    outs = []
    for g, win in enumerate(POOL_WINDOWS):
        xg = ug[:, :, g].astype(jnp.float32)
        csum = jnp.cumsum(xg, axis=1)
        lag = jnp.pad(csum[:, :L - win], ((0, 0), (win, 0), (0, 0)))
        count = jnp.minimum(jnp.arange(1, L + 1), win).astype(jnp.float32)
        outs.append((csum - lag) / count[None, :, None] - xg)
    d = jnp.stack(outs, axis=2).astype(u.dtype)
    y = jnp.einsum('blgc,gcd->blgd', d, w)
    return y.reshape(B, L, POOL_WIDTH) * scale

def banded(t, nc):
    B = t.shape[0]
    tc = t.reshape(B, nc, CHUNK, t.shape[2], t.shape[3])
    tp = jnp.pad(tc, ((0, 0), (WINDOW_CHUNKS - 1, 0), (0, 0), (0, 0), (0, 0)))
    return jnp.concatenate([tp[:, j:j + nc] for j in range(WINDOW_CHUNKS)], axis=2)

def swa_sinks(q, k, v, sinks):
    B, L, H, Dh = q.shape
    nc = L // CHUNK
    qc = q.reshape(B, nc, CHUNK, SWA_KV_HEADS, SWA_GROUP, Dh)
    kb, vb = banded(k, nc), banded(v, nc)
    s = jnp.einsum('bnqhgd,bnkhd->bnhgqk', qc, kb).astype(jnp.float32) * (Dh ** -0.5)
    key_chunk = (jnp.arange(nc)[:, None] - (WINDOW_CHUNKS - 1)
                 + jnp.arange(WINDOW_CHUNKS * CHUNK)[None, :] // CHUNK)
    valid = key_chunk >= 0
    s = jnp.where(valid[None, :, None, None, None, :], s, -jnp.inf)
    sink = sinks.astype(jnp.float32).reshape(SWA_KV_HEADS, SWA_GROUP)[None, None, :, :, None, None]
    m = jnp.maximum(jnp.max(s, axis=-1, keepdims=True), sink)
    p = jnp.exp(s - m)
    p = p / (jnp.sum(p, axis=-1, keepdims=True) + jnp.exp(sink - m))
    o = jnp.einsum('bnhgqk,bnkhd->bnqhgd', p.astype(v.dtype), vb)
    return o.reshape(B, L, H * Dh)

def layer_ab(h, w_in, w_out, lam_p, subln, pool_w, pool_scale, lambda_init, cos, sin):
    B, L, _ = h.shape
    proj = h @ w_in
    q, k, v, u, gate = jnp.split(
        proj, [DIFF_QK, 2 * DIFF_QK, 2 * DIFF_QK + DIFF_WIDTH,
               2 * DIFF_QK + DIFF_WIDTH + POOL_WIDTH], axis=-1)
    q = apply_rope(q.reshape(B, L, DIFF_HEADS, 2, DIFF_HEAD_DIM), cos, sin)
    k = apply_rope(k.reshape(B, L, DIFF_HEADS, 2, DIFF_HEAD_DIM), cos, sin)
    v = v.reshape(B, L, DIFF_HEADS, DIFF_V_DIM)
    lp = lam_p.astype(jnp.float32)
    lam = jnp.exp(jnp.sum(lp[0] * lp[1])) - jnp.exp(jnp.sum(lp[2] * lp[3])) + lambda_init
    a = diff_attention(q, k, v, lam)
    a = (rmsnorm(a, subln) * (1.0 - lambda_init)).reshape(B, L, DIFF_WIDTH)
    b = multiscale_pool(u, pool_w, pool_scale)
    y = jnp.concatenate([a, b], axis=-1) * jax.nn.silu(gate)
    return y @ w_out

def layer_c(h, w_in, w_out, sinks, cos, sin):
    B, L, _ = h.shape
    proj = h @ w_in
    q, k, v, gate = jnp.split(
        proj, [SWA_WIDTH, SWA_WIDTH + SWA_KV, SWA_WIDTH + 2 * SWA_KV], axis=-1)
    q = apply_rope(q.reshape(B, L, SWA_HEADS, SWA_HEAD_DIM), cos, sin)
    k = apply_rope(k.reshape(B, L, SWA_KV_HEADS, SWA_HEAD_DIM), cos, sin)
    v = v.reshape(B, L, SWA_KV_HEADS, SWA_HEAD_DIM)
    o = swa_sinks(q, k, v, sinks)
    return (o * jax.nn.silu(gate)) @ w_out

def setup_inputs(seed: int = 0) -> dict:
    key = jax.random.key(seed)
    ks = jax.random.split(key, 12)
    f32 = jnp.float32
    nrm = lambda k, shape, s: jax.random.normal(k, shape, f32) * s
    return {
        "x": nrm(ks[0], (BATCH, SEQ, D_MODEL), 1.0),
        "norm_pre": 1.0 + nrm(ks[1], (DEPTH, D_MODEL), 0.05),
        "norm_post": 1.0 + nrm(ks[2], (DEPTH, D_MODEL), 0.05),
        "ab_w_in": nrm(ks[3], (N_EVEN, D_MODEL, AB_IN), D_MODEL ** -0.5),
        "ab_w_out": nrm(ks[4], (N_EVEN, AB_WIDTH, D_MODEL), AB_WIDTH ** -0.5),
        "diff_lambda": nrm(ks[5], (N_EVEN, 4, DIFF_HEAD_DIM), 0.1),
        "diff_subln": 1.0 + nrm(ks[6], (N_EVEN, DIFF_V_DIM), 0.05),
        "pool_w": nrm(ks[7], (N_EVEN, POOL_GROUPS, POOL_GROUP_DIM, POOL_GROUP_DIM), POOL_GROUP_DIM ** -0.5),
        "pool_scale": 1.0 + nrm(ks[8], (N_EVEN, POOL_WIDTH), 0.1),
        "c_w_in": nrm(ks[9], (N_ODD, D_MODEL, C_IN), D_MODEL ** -0.5),
        "c_w_out": nrm(ks[10], (N_ODD, SWA_WIDTH, D_MODEL), SWA_WIDTH ** -0.5),
        "c_sinks": nrm(ks[11], (N_ODD, SWA_HEADS), 0.5),
    }

def reference(x, norm_pre, norm_post, ab_w_in, ab_w_out, diff_lambda, diff_subln,
              pool_w, pool_scale, c_w_in, c_w_out, c_sinks):
    cos, sin = rope_tables(x.shape[1], DIFF_HEAD_DIM)
    h = x
    for i in range(DEPTH):
        hn = rmsnorm(h, norm_pre[i])
        j = i // 2
        if i % 2 == 0:
            lambda_init = 0.8 - 0.6 * math.exp(-0.3 * i)
            y = layer_ab(hn, ab_w_in[j], ab_w_out[j], diff_lambda[j], diff_subln[j],
                         pool_w[j], pool_scale[j], lambda_init, cos, sin)
        else:
            y = layer_c(hn, c_w_in[j], c_w_out[j], c_sinks[j], cos, sin)
        h = h + rmsnorm(y, norm_post[i])
    return h


_drawn_inputs = setup_inputs


def setup_inputs(seed=0):
    import zlib

    import numpy as np

    out = dict(_drawn_inputs(seed))
    spreads = {}
    factors = {'c_sinks': 8.0}
    for name, (base, spread) in spreads.items():
        noise = np.random.default_rng([zlib.crc32(name.encode()), seed]).standard_normal(out[name].shape)
        drawn = base * np.exp(spread * noise) if base else spread * noise
        out[name] = __import__('jax').numpy.asarray(drawn.astype(out[name].dtype))
    for name, factor in factors.items():
        out[name] = (out[name] * factor).astype(out[name].dtype)
    return out
```

```python
from contextlib import ExitStack

import numpy as np

import concourse.bass as bass
from concourse import mybir

F32 = mybir.dt.float32
F32R = mybir.dt.float32r
ALU = mybir.AluOpType
ACT = mybir.ActivationFunctionType
AX = mybir.AxisListType

P = 128
SEQ = 2048
DM = 1024
KT = DM // P
TT = SEQ // P
SB = 512
NSB = SEQ // SB
EPS = 1e-6
ROPE_THETA = 10000.0

HEADS0 = 4
HD = 64
QK0, V0, U0 = 512, 512, 512
G0 = {"q": 0, "k": 4, "v": 8, "u": 12, "gate": 16}
G1 = {"q": 0, "k": 8, "v": 9, "gate": 10}
NG0, NG1 = 24, 18
WINDOWS = (2, 4, 8, 16)
LAMBDA_INIT = 0.2

PARTS0 = [(2, "query", "query"), (2, "rope", "rope"), (4, "plain", "plain"), (4, "silu", "silu")]
PARTS1 = [(4, "query", "query"), (1, "rope", "plain"), (4, "silu", "silu")]


def rope_tables():
    inv = (ROPE_THETA ** (-np.arange(0, HD, 2) / HD)).astype(np.float32)
    ang = np.arange(SEQ, dtype=np.float32)[None, :] * inv[:, None]
    cos, sin = np.cos(ang), np.sin(ang)
    return (np.ascontiguousarray(np.concatenate([cos, cos, cos, cos])),
            np.ascontiguousarray(np.concatenate([sin, -sin, sin, -sin])))


def pool_edge():
    t = np.zeros((P, len(WINDOWS), 16), np.float32)
    for g, w in enumerate(WINDOWS):
        t[:, g, :] = (np.float32(1.0) / np.minimum(np.arange(1, 17), w).astype(np.float32))[None, :]
    return t


class Core:

    def __init__(self):
        self.spent = []

    def semaphore(self, nc, ctx, name):
        made = ctx.enter_context(nc.semaphore(name))
        self.spent.append(made)
        return made

    def clear_spent(self, nc):
        with nc.Block() as block:
            @block.gpsimd
            def _(pool):
                for made in self.spent:
                    pool.sem_clear(made)
        self.spent = []


def bcast_row(vec, n):
    return vec.rearrange("(a n) -> a n", a=1).to_broadcast([P, n])


def phase_constants(nc, c, a):
    with ExitStack() as ctx:
        lam_in = ctx.enter_context(nc.sbuf_tensor("lam_in", [P, 4, HD], F32))
        lam_prod = ctx.enter_context(nc.sbuf_tensor("lam_prod", [P, 2, HD], F32))
        lam_sum = ctx.enter_context(nc.sbuf_tensor("lam_sum", [P, 2], F32))
        lam_exp = ctx.enter_context(nc.sbuf_tensor("lam_exp", [P, 2], F32))
        subln_in = ctx.enter_context(nc.sbuf_tensor("subln_in", [P, 1], F32))
        loaded = c.semaphore(nc, ctx, ("const_loaded"))
        zeroed = c.semaphore(nc, ctx, ("const_zeroed"))
        step = c.semaphore(nc, ctx, ("const_step"))
        exped = c.semaphore(nc, ctx, ("const_exped"))
        block = ctx.enter_context(nc.Block())

        @block.sync
        def _(sp):
            sp.dma_start(lam_in[:], a["diff_lambda"].rearrange("a n d -> a (n d)").to_broadcast([P, 4 * HD])
                         ).then_inc(loaded, 16)
            sp.dma_start(subln_in[:], a["diff_subln"].rearrange("a p -> p a")).then_inc(loaded, 16)
            sp.dma_start(c.pool_scale[:], a["pool_scale"].rearrange("a (g p) -> p (a g)", p=P),
                         allow_slow_non_contiguous=True).then_inc(loaded, 16)
            sp.dma_start(c.sinks[:], a["c_sinks"].to_broadcast([P, 16])).then_inc(loaded, 16)
            sp.wait_ge(loaded, 64)

        @block.gpsimd
        def _(pool):
            pool.memset(c.ident[:], 0.0).then_inc(zeroed, 1)
            pool.memset(c.ones[:], 1.0)
            pool.memset(c.eps[:], EPS)
            pool.memset(c.mask_q[:].bitcast(F32), 0.0).then_inc(zeroed, 1)
            pool.memset(c.mask_k[:].bitcast(F32), 0.0).then_inc(zeroed, 1)
            pool.memset(c.mask_all[:].bitcast(F32), 0.0).then_inc(zeroed, 1)
            pool.wait_ge(zeroed, 4)
            pool.memset(c.mask_q[0:1, 0:HD].bitcast(F32), 1.0)
            pool.memset(c.mask_all[0:1, :].bitcast(F32), 1.0)
            pool.memset(c.mask_k[0:1, :].bitcast(F32), -2.0 ** 120)
            pool.affine_select(out=c.ident[:], in_=c.ident[:], compare_op=ALU.not_equal, fill=1.0, base=0,
                               pattern=[[-1, P]], channel_multiplier=1).then_inc(zeroed, 1)

        @block.vector
        def _(dve):
            dve.memset(c.lower[0:HD, :], 0.0)
            dve.memset(c.lower[HD:P, :], 1.0)
            dve.wait_ge(loaded, 64)
            dve.tensor_tensor(lam_prod[:], lam_in[:, 0:4:2], lam_in[:, 1:4:2], ALU.mult).then_inc(step, 1)
            dve.wait_ge(step, 1)
            dve.reduce_sum(lam_sum[:], lam_prod[:], AX.X).then_inc(step, 1)
            dve.tensor_scalar(c.subln[:], subln_in[:], 1.0 - LAMBDA_INIT, None, ALU.mult)
            dve.memset(c.lam[:, 0:1], 1.0)
            dve.wait_ge(exped, 1)
            dve.scalar_tensor_tensor(c.lam[:, 1:2], lam_exp[:, 1:2], LAMBDA_INIT, lam_exp[:, 0:1],
                                     ALU.subtract, ALU.subtract).then_inc(step, 1)
            dve.wait_ge(step, 3)

        @block.scalar
        def _(act):
            act.wait_ge(step, 2)
            act.activation(lam_exp[:], lam_sum[:], ACT.Exp).then_inc(exped, 1)


def norm_and_transpose(nc, c, src, gain, hn_hi, hn_lo):
    with ExitStack() as ctx:
        def sb(name, shape, dt=F32):
            return ctx.enter_context(nc.sbuf_tensor(name, shape, dt))

        def sem(name):
            return c.semaphore(nc, ctx, (name))

        x = [sb(f"nx{b}", [P, DM]) for b in range(2)]
        xs = [sb(f"nxs{b}", [P, DM]) for b in range(2)]
        square = sb("nsquare", [P, DM])
        g = sb("ngain", [P, DM])
        ss = [sb(f"nss{b}", [P, 1]) for b in range(2)]
        ln = [sb(f"nln{b}", [P, 1]) for b in range(2)]
        rstd = [sb(f"nrstd{b}", [P, 1]) for b in range(2)]
        g_loaded = sem("g_loaded")
        x_loaded = [sem(f"x_loaded{b}") for b in range(2)]
        stat = sem("norm_stat")
        rstd_ready = [sem(f"rstd_ready{b}") for b in range(2)]
        scaled = [sem(f"x_scaled{b}") for b in range(2)]
        turned = [sem(f"x_turned{b}") for b in range(2)]
        hi_ready = [sem(f"hn_hi_ready{b}") for b in range(2)]
        lo_ready = [sem(f"hn_lo_ready{b}") for b in range(2)]
        block = ctx.enter_context(nc.Block())
        tiles = src.rearrange("(t p) d -> t p d", p=P)

        def bank(b, h):
            return c.bank[2 * b + h]

        def cols(t, h):
            return slice(None), slice(4 * h, 4 * h + 4), bass.ds(t * P, P)

        @block.sync
        def _(sp):
            sp.dma_start(g[:], bcast_row(gain, DM)).then_inc(g_loaded, 16)
            for b in range(2):
                sp.dma_start(x[b][:], tiles[b]).then_inc(x_loaded[b], 16)
            with sp.Fori(0, TT // 2 - 1) as i:
                for b in range(2):
                    sp.wait_ge(scaled[b], i + 1)
                    sp.dma_start(x[b][:], tiles[2 * i + 2 + b]).then_inc(x_loaded[b], 16)

        @block.scalar
        def _(act):
            def stats(b, i, n):
                act.wait_ge(x_loaded[b], 16 * (i + 1))
                act.activation(square[:], x[b][:], ACT.Square, accum_out=ss[b][:]).then_inc(stat, 1)
                act.wait_ge(stat, n + 1)
                act.activation(ln[b][:], ss[b][:], ACT.Ln, bias=c.eps[:], scale=1.0 / DM).then_inc(stat, 1)
                act.wait_ge(stat, n + 2)
                act.activation(rstd[b][:], ln[b][:], ACT.Exp, scale=-0.5).then_inc(rstd_ready[b], 1)

            def evacuate(b, i, t):
                act.wait_ge(turned[b], i + 1)
                act.activation(hn_hi[cols(t, 0)], bank(b, 0)[:].rearrange("p (k n) -> p k n", k=4), ACT.Copy)
                act.activation(hn_hi[cols(t, 1)], bank(b, 1)[:].rearrange("p (k n) -> p k n", k=4), ACT.Copy
                               ).then_inc(hi_ready[b], 1)

            stats(0, 0, 0)
            with act.Fori(0, TT // 2 - 1) as i:
                stats(1, i, 4 * i + 2)
                evacuate(0, i, 2 * i)
                stats(0, i + 1, 4 * i + 4)
                evacuate(1, i, 2 * i + 1)
            last = TT // 2 - 1
            stats(1, last, 4 * last + 2)
            evacuate(0, last, 2 * last)
            evacuate(1, last, 2 * last + 1)

        @block.vector
        def _(dve):
            def scale(b, i):
                dve.wait_ge(rstd_ready[b], i + 1)
                dve.wait_ge(turned[b], i + 1)
                dve.scalar_tensor_tensor(xs[b][:], x[b][:], rstd[b][:], g[:], ALU.mult, ALU.mult
                                         ).then_inc(scaled[b], 1)

            def evacuate(b, i, t):
                dve.wait_ge(hi_ready[b], i + 1)
                for h in range(2):
                    lo = dve.tensor_tensor(hn_lo[cols(t, h)], bank(b, h)[:].rearrange("p (k n) -> p k n", k=4),
                                           hn_hi[cols(t, h)].bitcast(F32), ALU.subtract)
                lo.then_inc(lo_ready[b], 1)

            dve.wait_ge(g_loaded, 16)
            dve.wait_ge(rstd_ready[0], 1)
            dve.scalar_tensor_tensor(xs[0][:], x[0][:], rstd[0][:], g[:], ALU.mult, ALU.mult).then_inc(scaled[0], 1)
            dve.wait_ge(rstd_ready[1], 1)
            dve.scalar_tensor_tensor(xs[1][:], x[1][:], rstd[1][:], g[:], ALU.mult, ALU.mult).then_inc(scaled[1], 1)
            with dve.Fori(0, TT // 2 - 1) as i:
                for b in range(2):
                    evacuate(b, i, 2 * i + b)
                    dve.wait_ge(rstd_ready[b], i + 2)
                    dve.scalar_tensor_tensor(xs[b][:], x[b][:], rstd[b][:], g[:], ALU.mult, ALU.mult
                                             ).then_inc(scaled[b], 1)
            last = TT // 2 - 1
            for b in range(2):
                evacuate(b, last, 2 * last + b)

        @block.tensor
        def _(pe):
            def turn(b, i):
                pe.wait_ge(scaled[b], i + 1)
                for k in range(KT):
                    tr = pe.transpose(bank(b, k // 4)[:, (k % 4) * P:(k % 4 + 1) * P],
                                      xs[b][:, k * P:(k + 1) * P], c.ident[:])
                tr.then_inc(turned[b], 1)

            turn(0, 0)
            turn(1, 0)
            with pe.Fori(1, TT // 2) as i:
                for b in range(2):
                    pe.wait_ge(lo_ready[b], i)
                    turn(b, i)


def in_projection(nc, name, c, w, hn_hi, hn_lo, parts, out, load=None):
    groups = sum(2 * n for n, _, _ in parts)
    w_groups = w.rearrange("(k p) n -> p k n", p=P)
    with ExitStack() as ctx:
        def sb(nm, shape, dt=F32):
            return ctx.enter_context(nc.sbuf_tensor(f"{name}_{nm}", shape, dt))

        def sem(nm):
            return c.semaphore(nc, ctx, (f"{name}_{nm}"))

        cos, sin = sb("cos", [P, SEQ]), sb("sin", [P, SEQ])
        w_raw = [sb(f"w_raw{b}", [P, KT, P]) for b in range(2)]
        w_hi = [sb(f"w_hi{b}", [P, KT, P], F32R) for b in range(2)]
        w_lo = [sb(f"w_lo{b}", [P, KT, P], F32R) for b in range(2)]
        stage = [sb(f"stage{s}", [P, SB]) for s in range(NSB)]
        direct = [sb(f"direct{r}", [P, SB]) for r in range(2)]
        rotated = [sb(f"rotated{r}", [P, SB]) for r in range(2)]
        tables = sem("tables_loaded")
        hn_loaded = [sem(f"hn_loaded{s}") for s in range(NSB)]
        w_loaded = [sem(f"w_loaded{b}") for b in range(2)]
        hi_ready = [sem(f"w_hi_ready{b}") for b in range(2)]
        lo_ready = [sem(f"w_lo_ready{b}") for b in range(2)]
        product = [sem(f"product{b}") for b in range(2)]
        bank_free = [sem(f"bank_free{b}") for b in range(2)]
        roped = sem("roped")
        stored = [sem(f"stored{s}") for s in range(NSB)]
        block = ctx.enter_context(nc.Block())

        def walk(eng, step, first=0):
            done, ropes = 0, 0
            for at, (pairs, even, odd) in enumerate(parts):
                looped = pairs - 1 if at == len(parts) - 1 else pairs
                turned = [kind in ("query", "rope") for kind in (even, odd)]
                per = sum(turned)

                def pair(i, last):
                    for b, kind in enumerate((even, odd)):
                        m = done // 2 + i
                        r = ropes + per * i + (b if turned[0] else 0)
                        step(2 * m + b, m, b, r, kind, last)

                if looped == 1:
                    pair(0, False)
                else:
                    with eng.Fori(0, looped) as i:
                        pair(i, False)
                if looped < pairs:
                    pair(looped, True)
                done += 2 * pairs
                ropes += per * pairs

        @block.sync
        def _(sp):
            for s in range(NSB):
                sp.sem_inc(stored[s], 16)

            def load_w(n, b):
                sp.dma_start(w_raw[b][:], w_groups[:, :, bass.ds(n * P, P)]).then_inc(w_loaded[b], 16)

            for b in range(2):
                load_w(b, b)
            if load is not None:
                for s in range(NSB):
                    for half in range(SB // SD):
                        tok = slice(s * SB + half * SD, s * SB + (half + 1) * SD)
                        for dst, srct in ((hn_hi, load[0]), (hn_lo, load[1])):
                            sp.dma_start(dst[:, :, tok].bitcast(F32), srct[s * SB // SD + half].bitcast(F32)
                                         ).then_inc(hn_loaded[s], 16)
            sp.dma_start(cos[:], c.rope_cos).then_inc(tables, 16)
            sp.dma_start(sin[:], c.rope_sin).then_inc(tables, 16)

            def step(n, m, b, r, kind, last):
                if not last:
                    sp.wait_ge(lo_ready[b], m + 1)
                    load_w(n + 2, b)
                for s in range(NSB):
                    if kind in ("query", "rope"):
                        sp.wait_ge(roped, 4 * r + s + 3)
                    else:
                        sp.wait_ge(bank_free[b], 4 * m + s + 5)
                    sp.dma_start(out[n, :, s * SB:(s + 1) * SB], stage[s][:]).then_inc(stored[s], 16)

            walk(sp, step)
            for s in range(NSB):
                sp.wait_ge(stored[s], 16 * (groups + 1))

        @block.scalar
        def _(act):
            for b in range(2):
                act.sem_inc(bank_free[b], NSB)

            def split(m, b):
                act.wait_ge(w_loaded[b], 16 * (m + 1))
                act.activation(w_hi[b][:], w_raw[b][:], ACT.Copy).then_inc(hi_ready[b], 1)

            split(0, 0)
            act.wait_ge(w_loaded[1], 16)
            act.activation(w_hi[1][:], w_raw[1][:], ACT.Copy).then_inc(hi_ready[1], 1)

            def step(n, m, b, r, kind, last):
                for s in range(NSB):
                    if kind not in ("query", "rope"):
                        act.wait_ge(product[b], 4 * m + s + 1)
                        act.wait_ge(stored[s], 16 * (n + 1))
                        act.activation(stage[s][:], c.bank[4 * b + s][:],
                                       ACT.Silu if kind == "silu" else ACT.Copy).then_inc(bank_free[b], 1)
                if not last:
                    act.wait_ge(product[b], 4 * m + 4)
                    split(m + 1, b)

            walk(act, step)

        @block.gpsimd
        def _(pool):
            pool.sem_inc(roped, 2)

            def split(m, b):
                pool.wait_ge(hi_ready[b], m + 1)
                pool.tensor_tensor(w_lo[b][:], w_raw[b][:], w_hi[b][:].bitcast(F32), ALU.subtract
                                   ).then_inc(lo_ready[b], 1)

            split(0, 0)
            split(0, 1)

            def step(n, m, b, r, kind, last):
                if kind in ("query", "rope"):
                    for s in range(NSB):
                        pool.wait_ge(bank_free[b], 4 * m + s + 5)
                        pool.wait_ge(stored[s], 16 * (n + 1))
                        pool.tensor_tensor(stage[s][:], direct[s % 2][:], rotated[s % 2][:], ALU.add
                                           ).then_inc(roped, 1)
                if not last:
                    split(m + 1, b)

            walk(pool, step)

        @block.vector
        def _(dve):
            dve.wait_ge(tables, 32)

            def step(n, m, b, r, kind, last):
                if kind not in ("query", "rope"):
                    return
                for s in range(NSB):
                    dve.wait_ge(product[b], 4 * m + s + 1)
                    dve.wait_ge(roped, 4 * r + s + 1)
                    bank = c.bank[4 * b + s]
                    tok = slice(s * SB, (s + 1) * SB)
                    factor = HD ** -0.5 if kind == "query" else 1.0
                    dve.scalar_tensor_tensor(direct[s % 2][:], bank[:], factor, cos[:, tok], ALU.mult, ALU.mult)
                    for src, dst in ((0, 32), (32, 0), (64, 96), (96, 64)):
                        rot = dve.scalar_tensor_tensor(rotated[s % 2][dst:dst + 32, :], bank[src:src + 32, :], factor,
                                                       sin[src:src + 32, tok], ALU.mult, ALU.mult)
                    rot.then_inc(bank_free[b], 1)

            walk(dve, step)

        @block.tensor
        def _(pe):
            def step(n, m, b, r, kind, last):
                pe.wait_ge(lo_ready[b], m + 1)
                for s in range(NSB):
                    pe.wait_ge(bank_free[b], 4 * m + s + 1)
                    tok = slice(s * SB, (s + 1) * SB)
                    for k in range(KT):
                        bank = c.bank[4 * b + s][:]
                        pe.matmul(bank, w_hi[b][:, k], hn_hi[:, k, tok], start=(k == 0), stop=False)
                        pe.matmul(bank, w_hi[b][:, k], hn_lo[:, k, tok], start=False, stop=False)
                        mm = pe.matmul(bank, w_lo[b][:, k], hn_hi[:, k, tok], start=False, stop=(k == KT - 1))
                    mm.then_inc(product[b], 1)

            if load is not None:
                for s in range(NSB):
                    pe.wait_ge(hn_loaded[s], 64)
            walk(pe, step)


def differential_attention(nc, c, proj, o_out):
    CH = 512
    STEPS = 2 * TT // 2
    UNITS = 2 * TT

    def chunks(u):
        keys = (u % TT + 1) * P
        return [(at, min(CH, keys - at)) for at in range(0, keys, CH)]

    chunk_base = [sum(len(chunks(v)) for v in range(u)) for u in range(UNITS + 1)]
    CHUNKS = chunk_base[UNITS]
    turn_of, turns = {}, 0
    turn_of["v", 0] = turns
    turns += 1
    for u in range(UNITS + 2):
        if u % 2 == 1 and u // 2 + 1 < STEPS:
            turn_of["v", u // 2 + 1] = turns
            turns += 1
        if u >= 2:
            for n in range(len(chunks(u - 2))):
                turn_of[u - 2, n] = turns
                turns += 1

    with ExitStack() as ctx:
        def sb(name, shape, dt=F32):
            return ctx.enter_context(nc.sbuf_tensor("da_" + name, shape, dt))

        def sem(name):
            return c.semaphore(nc, ctx, ("da_" + name))

        raw_k = [sb(f"raw_k{r}", [P, 2, 2 * P]) for r in range(2)]
        raw_q = [sb(f"raw_q{r}", [P, 2, 2 * P]) for r in range(2)]
        raw_v = [sb(f"raw_v{r}", [P, 2 * P]) for r in range(2)]
        k_stack = [sb(f"k_stack{h}", [P, 2, SEQ], F32R) for h in range(2)]
        k_take = [sb(f"k_take{r}", [P, 2, 2 * P]) for r in range(2)]
        q_hi = [sb(f"q_hi{r}", [P, 2, 2 * P], F32R) for r in range(2)]
        q_lo = [sb(f"q_lo{r}", [P, 2, 2 * P], F32R) for r in range(2)]
        v_hi = [sb(f"v_hi{h}", [P, TT, P], F32R) for h in range(2)]
        v_lo = [sb(f"v_lo{h}", [P, TT, P], F32R) for h in range(2)]
        probs = [sb(f"probs{r}", [P, 2, SEQ]) for r in range(3)]
        wt_hi = [sb(f"wt_hi{r}", [P, TT, 2 * P], F32R) for r in range(2)]
        wt_lo = [sb(f"wt_lo{r}", [P, TT, 2 * P], F32R) for r in range(2)]
        o_stage = [sb(f"o_stage{r}", [P, 2 * P]) for r in range(2)]
        neg_max = [sb(f"neg_max{r}", [P, 2, 4]) for r in range(2)]
        sums = [sb(f"sums{r}", [P, 2, 4]) for r in range(2)]
        least = [sb(f"least{r}", [P, 2]) for r in range(2)]
        shift = [sb(f"shift{r}", [P, 2, 4]) for r in range(2)]
        factor = [sb(f"factor{r}", [P, 2, 4]) for r in range(2)]
        part = [sb(f"part{r}", [P, 2, 4]) for r in range(2)]
        total = [sb(f"total{r}", [P, 2]) for r in range(2)]
        inverse = [sb(f"inverse{r}", [P, 2]) for r in range(2)]
        signed = [sb(f"signed{r}", [P, 2]) for r in range(2)]
        weight = [sb(f"weight{r}", [P, 2, 4]) for r in range(2)]

        raw_loaded = [sem(f"raw_loaded{r}") for r in range(2)]
        split_hi = sem("split_hi")
        split_lo = sem("split_lo")
        scores = sem("scores")
        maxed = sem("maxed")
        exped = sem("exped")
        shifted = sem("shifted")
        factored = sem("factored")
        stat = sem("stat")
        weighted = sem("weighted")
        second = sem("second")
        joined = sem("joined")
        turned = sem("turned")
        turned_hi = sem("turned_hi")
        turned_lo = sem("turned_lo")
        output = sem("output")
        staged = sem("staged")
        stored = [sem(f"stored{r}") for r in range(2)]
        sp_passed, pool_passed = sem("sp_passed"), sem("pool_passed")
        block = ctx.enter_context(nc.Block())
        s_bank, t_bank, o_bank = c.bank[0:4], c.bank[4:6], c.bank[6:8]
        LOADS = 80

        STATS = sum(5 if len(chunks(u)) > 1 else 1 for u in range(UNITS))
        stat_base = [sum(5 if len(chunks(v)) > 1 else 1 for v in range(u)) for u in range(UNITS + 1)]
        long_units = [u for u in range(UNITS) if len(chunks(u)) > 1]

        @block.sync
        def _(sp):
            for r in range(2):
                sp.sem_inc(stored[r], 16)
            with sp.Fori(0, 2) as i:
                def load(g):
                    h, j, r = g // 8, g % 8, g % 2
                    tok = slice(j * 2 * P, (j + 1) * 2 * P)
                    head = 2 * i + h
                    for half in range(2):
                        rows = slice(half * HD, (half + 1) * HD)
                        for dst, first in ((raw_k, G0["k"]), (raw_q, G0["q"])):
                            sp.dma_start(dst[r][rows], proj[first + head].rearrange("(m p) t -> p m t", m=2)[:, :, tok]
                                         ).then_inc(raw_loaded[r], 16)
                    sp.dma_start(raw_v[r][:], proj[G0["v"] + head, :, tok]).then_inc(raw_loaded[r], 16)

                def store(g):
                    h, j = g // 8, g % 8
                    sp.wait_ge(staged, STEPS * i + g + 1)
                    sp.sem_inc(sp_passed, 1)
                    sp.dma_start(o_out[2 * i + h, :, j * 2 * P:(j + 1) * 2 * P], o_stage[g % 2][:]
                                 ).then_inc(stored[g % 2], 16)

                load(0)
                load(1)
                for g in range(2, STEPS + 4):
                    if g < STEPS:
                        sp.wait_ge(split_lo, STEPS * i + g - 1)
                        sp.sem_inc(sp_passed, 1)
                        sp.wait_ge(turned, turns * i + turn_of["v", g - 2] + 1)
                        sp.sem_inc(sp_passed, 1)
                        load(g)
                    if g >= 4:
                        store(g - 4)
            for r in range(2):
                sp.wait_ge(stored[r], 16 * (STEPS + 1))

        @block.gpsimd
        def _(pool):
            with pool.Fori(0, 2) as i:
                def split(g):
                    h, j, r = g // 8, g % 8, g % 2
                    tok = slice(j * 2 * P, (j + 1) * 2 * P)
                    pool.wait_ge(split_hi, STEPS * i + g + 1)
                    pool.tensor_tensor(q_lo[r][:], raw_q[r][:], q_hi[r][:].bitcast(F32), ALU.subtract)
                    pool.tensor_tensor(k_stack[h][:, :, tok], raw_k[r][:], k_take[r][:], ALU.subtract
                                       ).then_inc(split_lo, 1)

                split(0)
                for u in range(UNITS + 1):
                    if u % 2 == 1 and u // 2 + 1 < STEPS:
                        split(u // 2 + 1)
                    if u >= 1:
                        v = u - 1
                        pool.wait_ge(weighted, UNITS * i + v + 1)
                        pool.sem_inc(pool_passed, 1)
                        for n, (at, keys) in enumerate(chunks(v)):
                            span = probs[v % 3][:, 1, at:at + keys]
                            pool.tensor_scalar(span, span, weight[v % 2][:, 1, n:n + 1], 1.0, ALU.mult, ALU.mult
                                               ).then_inc(second, 1)

        @block.scalar
        def _(act):
            with act.Fori(0, 2) as i:
                def split(g):
                    h, j, r = g // 8, g % 8, g % 2
                    tok = slice(j * 2 * P, (j + 1) * 2 * P)
                    act.wait_ge(raw_loaded[r], LOADS * (STEPS // 2) * i + LOADS * (g // 2 + 1))
                    if g >= 2:
                        act.wait_ge(scores, 2 * CHUNKS * i + 2 * chunk_base[2 * g - 2])
                    act.activation(q_hi[r][:], raw_q[r][:], ACT.Copy)
                    act.activation(k_take[r][:].bitcast(F32R), raw_k[r][:], ACT.Copy, scale=c.lower[:]).then_inc(split_hi, 1)

                def values_hi(g):
                    t = turn_of["v", g]
                    act.wait_ge(turned, turns * i + t + 1)
                    act.activation(v_hi[g // 8][:, 2 * (g % 8):2 * (g % 8) + 2, :],
                                   t_bank[t % 2][:, 0:2 * P].rearrange("p (k n) -> p k n", n=P), ACT.Copy
                                   ).then_inc(turned_hi, 1)

                def factors(u):
                    if len(chunks(u)) > 1:
                        act.wait_ge(shifted, len(long_units) * i + long_units.index(u) + 1)
                        act.activation(factor[u % 2][:, :, 0:len(chunks(u))], shift[u % 2][:, :, 0:len(chunks(u))],
                                       ACT.Exp).then_inc(factored, 1)

                def exponentials(u, n):
                    at, keys = chunks(u)[n]
                    for m in range(2):
                        s = 2 * (chunk_base[u] + n) + m
                        if n == 0 and m == 0 and u >= 3:
                            last = len(chunks(u - 3)) - 1
                            act.wait_ge(turned, turns * i + turn_of[u - 3, last] + 1)
                        act.wait_ge(maxed, 2 * CHUNKS * i + s + 1)
                        act.activation(probs[u % 3][:, m, at:at + keys], s_bank[s % 4][:, 0:keys], ACT.Exp,
                                       bias=neg_max[u % 2][:, m, n:n + 1], accum_out=sums[u % 2][:, m, n:n + 1]
                                       ).then_inc(exped, 1)

                def weights_hi(u, n):
                    at, keys = chunks(u)[n]
                    t = turn_of[u, n]
                    if n == 0 and u % 2 == 0 and u >= 4:
                        act.wait_ge(output, STEPS * i + u // 2 - 1)
                    act.wait_ge(turned, turns * i + t + 1)
                    act.activation(wt_hi[u // 2 % 2][:, at // P:(at + keys) // P, (u % 2) * P:(u % 2 + 1) * P],
                                   t_bank[t % 2][:, 0:keys].rearrange("p (k n) -> p k n", n=P), ACT.Copy
                                   ).then_inc(turned_hi, 1)

                def take_output(g):
                    act.wait_ge(output, STEPS * i + g + 1)
                    act.wait_ge(stored[g % 2], 16 * (STEPS // 2) * i + 16 * (g // 2 + 1))
                    act.activation(o_stage[g % 2][:], o_bank[g % 2][:, 0:2 * P], ACT.Copy).then_inc(staged, 1)

                split(0)
                values_hi(0)
                for u in range(UNITS + 2):
                    if u % 2 == 1 and u // 2 + 1 < STEPS:
                        split(u // 2 + 1)
                        values_hi(u // 2 + 1)
                    if 1 <= u <= UNITS:
                        factors(u - 1)
                    for n in range(4):
                        if u < UNITS and n < len(chunks(u)):
                            exponentials(u, n)
                        if u >= 2 and n < len(chunks(u - 2)):
                            weights_hi(u - 2, n)
                    if u % 2 == 1 and u >= 5:
                        take_output((u - 5) // 2)
                take_output(STEPS - 1)

        @block.vector
        def _(dve):
            with dve.Fori(0, 2) as i:
                def values_lo(g):
                    t = turn_of["v", g]
                    tiles = slice(2 * (g % 8), 2 * (g % 8) + 2)
                    dve.wait_ge(turned_hi, turns * i + t + 1)
                    dve.tensor_tensor(v_lo[g // 8][:, tiles, :], t_bank[t % 2][:, 0:2 * P].rearrange("p (k n) -> p k n", n=P),
                                      v_hi[g // 8][:, tiles, :].bitcast(F32), ALU.subtract).then_inc(turned_lo, 1)

                def chain(ins, u, n):
                    ins.then_inc(stat, 1)
                    dve.wait_ge(stat, STATS * i + stat_base[u] + n)

                def weights(u):
                    r, k = u % 2, len(chunks(u))
                    dve.wait_ge(exped, 2 * CHUNKS * i + 2 * chunk_base[u + 1])
                    if k > 1:
                        dve.wait_ge(factored, len(long_units) * i + long_units.index(u) + 1)
                        chain(dve.tensor_tensor(part[r][:, :, 0:k], factor[r][:, :, 0:k], sums[r][:, :, 0:k], ALU.mult), u, 2)
                        chain(dve.reduce_sum(total[r][:], part[r][:, :, 0:k], AX.X), u, 3)
                        chain(dve.reciprocal(inverse[r][:], total[r][:]), u, 4)
                        chain(dve.tensor_tensor(signed[r][:], inverse[r][:], c.lam[:], ALU.mult), u, 5)
                        dve.tensor_tensor(weight[r][:, :, 0:k], factor[r][:, :, 0:k],
                                          signed[r][:].unsqueeze(2).to_broadcast([P, 2, k]), ALU.mult).then_inc(weighted, 1)
                    else:
                        chain(dve.reciprocal(inverse[r][:], sums[r][:, :, 0]), u, 1)
                        dve.tensor_tensor(weight[r][:, :, 0], inverse[r][:], c.lam[:], ALU.mult).then_inc(weighted, 1)

                def maxima(u, n):
                    at, keys = chunks(u)[n]
                    for m in range(2):
                        s = 2 * (chunk_base[u] + n) + m
                        dve.wait_ge(scores, 2 * CHUNKS * i + s + 1)
                        dve.tensor_reduce(neg_max[u % 2][:, m, n:n + 1], s_bank[s % 4][:, 0:keys], AX.X, ALU.max,
                                          negate=True).then_inc(maxed, 1)

                def shifts(u):
                    r, k = u % 2, len(chunks(u))
                    if k > 1:
                        dve.wait_ge(maxed, 2 * CHUNKS * i + 2 * chunk_base[u + 1])
                        chain(dve.tensor_reduce(least[r][:], neg_max[r][:, :, 0:k], AX.X, ALU.min), u, 1)
                        dve.tensor_tensor(shift[r][:, :, 0:k], least[r][:].unsqueeze(2).to_broadcast([P, 2, k]),
                                          neg_max[r][:, :, 0:k], ALU.subtract).then_inc(shifted, 1)

                def join(u, n):
                    at, keys = chunks(u)[n]
                    if n == 0:
                        dve.wait_ge(weighted, UNITS * i + u + 1)
                    dve.wait_ge(second, CHUNKS * i + chunk_base[u] + n + 1)
                    first, other = probs[u % 3][:, 0, at:at + keys], probs[u % 3][:, 1, at:at + keys]
                    dve.scalar_tensor_tensor(first, first, weight[u % 2][:, 0, n:n + 1], other, ALU.mult, ALU.add
                                             ).then_inc(joined, 1)

                def weights_lo(u, n):
                    at, keys = chunks(u)[n]
                    t = turn_of[u, n]
                    where = (slice(None), slice(at // P, (at + keys) // P), slice((u % 2) * P, (u % 2 + 1) * P))
                    dve.wait_ge(turned_hi, turns * i + t + 1)
                    dve.tensor_tensor(wt_lo[u // 2 % 2][where], t_bank[t % 2][:, 0:keys].rearrange("p (k n) -> p k n", n=P),
                                      wt_hi[u // 2 % 2][where].bitcast(F32), ALU.subtract).then_inc(turned_lo, 1)

                values_lo(0)
                for u in range(UNITS + 2):
                    if u % 2 == 1 and u // 2 + 1 < STEPS:
                        values_lo(u // 2 + 1)
                    if 1 <= u <= UNITS:
                        weights(u - 1)
                    for n in range(4):
                        if u < UNITS and n < len(chunks(u)):
                            maxima(u, n)
                        if 1 <= u <= UNITS and n < len(chunks(u - 1)):
                            join(u - 1, n)
                        if u >= 2 and n < len(chunks(u - 2)):
                            weights_lo(u - 2, n)
                    if u < UNITS:
                        shifts(u)

        @block.tensor
        def _(pe):
            with pe.Fori(0, 2) as i:
                def turn_bank(t):
                    if t >= 2:
                        pe.wait_ge(turned_lo, turns * i + t - 1)

                def turn_values(g):
                    t = turn_of["v", g]
                    pe.wait_ge(raw_loaded[g % 2], LOADS * (STEPS // 2) * i + LOADS * (g // 2 + 1))
                    turn_bank(t)
                    for k in range(2):
                        tr = pe.transpose(t_bank[t % 2][:, k * P:(k + 1) * P], raw_v[g % 2][:, k * P:(k + 1) * P], c.ident[:])
                    tr.then_inc(turned, 1)

                def score(u, n):
                    h, g = u // TT, u // 2
                    at, keys = chunks(u)[n]
                    queries = slice((u % 2) * P, (u % 2 + 1) * P)
                    if n == 0 and u % 2 == 0:
                        pe.wait_ge(split_lo, STEPS * i + g + 1)
                    for m in range(2):
                        s = 2 * (chunk_base[u] + n) + m
                        if s >= 4:
                            pe.wait_ge(exped, 2 * CHUNKS * i + s - 3)
                        bank = s_bank[s % 4]
                        keys_moving = k_stack[h][:, m, at:at + keys]
                        pe.matmul(bank[:, 0:keys], q_hi[g % 2][:, m, queries], keys_moving, start=True, stop=False)
                        if at + keys == (u % TT + 1) * P:
                            pe.matmul(bank[:, keys - HD:keys], c.mask_q[:], c.mask_k[:], start=False, stop=False)
                        pe.matmul(bank[:, 0:keys], q_lo[g % 2][:, m, queries], keys_moving, start=False, stop=True
                                  ).then_inc(scores, 1)

                def turn_weights(u, n):
                    at, keys = chunks(u)[n]
                    t = turn_of[u, n]
                    pe.wait_ge(joined, CHUNKS * i + chunk_base[u] + n + 1)
                    turn_bank(t)
                    for k in range(keys // P):
                        tr = pe.transpose(t_bank[t % 2][:, k * P:(k + 1) * P],
                                          probs[u % 3][:, 0, at + k * P:at + (k + 1) * P], c.ident[:])
                    tr.then_inc(turned, 1)

                def values(g):
                    h, j, r = g // 8, g % 8, g % 2
                    if g >= 2:
                        pe.wait_ge(staged, STEPS * i + g - 1)
                    last = turn_of[2 * g + 1, len(chunks(2 * g + 1)) - 1]
                    pe.wait_ge(turned_lo, turns * i + last + 1)
                    tiles = 2 * j + 2
                    for k in range(tiles):
                        q = slice(P if k == tiles - 1 else 0, 2 * P)
                        out = o_bank[r][:, q]
                        pe.matmul(out, v_hi[h][:, k], wt_hi[r][:, k, q], start=(k == 0), stop=False)
                        pe.matmul(out, v_hi[h][:, k], wt_lo[r][:, k, q], start=False, stop=False)
                        mm = pe.matmul(out, v_lo[h][:, k], wt_hi[r][:, k, q], start=False, stop=(k == tiles - 1))
                    mm.then_inc(output, 1)

                turn_values(0)
                for u in range(UNITS + 2):
                    if u % 2 == 1 and u // 2 + 1 < STEPS:
                        turn_values(u // 2 + 1)
                    for n in range(4):
                        if u < UNITS and n < len(chunks(u)):
                            score(u, n)
                        if u >= 2 and n < len(chunks(u - 2)):
                            turn_weights(u - 2, n)
                    if u % 2 == 0 and u >= 4:
                        values((u - 4) // 2)
                values(STEPS - 1)


def pooling(nc, c, proj, w, edge, b_out):
    PAD = 16
    NGR = len(WINDOWS)
    with ExitStack() as ctx:
        def sb(name, shape, dt=F32):
            return ctx.enter_context(nc.sbuf_tensor("pl_" + name, shape, dt))

        def sem(name):
            return c.semaphore(nc, ctx, ("pl_" + name))

        u = [sb(f"u{r}", [P, PAD + SEQ]) for r in range(2)]
        run = [sb(f"run{r}", [P, PAD + SEQ]) for r in range(2)]
        diff = [sb(f"diff{r}", [P, SEQ]) for r in range(2)]
        d_hi = [sb(f"d_hi{r}", [P, SEQ], F32R) for r in range(2)]
        d_lo = [sb(f"d_lo{r}", [P, SEQ], F32R) for r in range(2)]
        w_raw, w_hi, w_lo = sb("w_raw", [P, NGR, P]), sb("w_hi", [P, NGR, P], F32R), sb("w_lo", [P, NGR, P], F32R)
        edges = sb("edges", [P, NGR, 16])
        stage = [sb(f"stage{r}", [P, SB]) for r in range(4)]
        cleared, consts = sem("cleared"), sem("consts")
        u_loaded = [sem(f"u_loaded{r}") for r in range(2)]
        chained, differed = sem("chained"), sem("differed")
        hi_ready, lo_ready = sem("hi_ready"), sem("lo_ready")
        w_hi_ready, w_lo_ready = sem("w_hi_ready"), sem("w_lo_ready")
        product, staged = sem("product"), sem("staged")
        stored = [sem(f"stored{r}") for r in range(4)]
        block = ctx.enter_context(nc.Block())

        @block.sync
        def _(sp):
            sp.dma_start(w_raw[:], w.rearrange("g c d -> c g d")).then_inc(consts, 16)
            sp.dma_start(edges[:], edge).then_inc(consts, 16)
            for g in range(NGR):
                if g >= 2:
                    sp.wait_ge(differed, g - 1)
                sp.dma_start(u[g % 2][:, PAD:], proj[G0["u"] + g]).then_inc(u_loaded[g % 2], 16)
            for g in range(NGR):
                for s in range(NSB):
                    sp.wait_ge(staged, NSB * g + s + 1)
                    sp.dma_start(b_out[g, :, s * SB:(s + 1) * SB], stage[s][:]).then_inc(stored[s], 16)
            for s in range(NSB):
                sp.wait_ge(stored[s], 16 * NGR)

        @block.gpsimd
        def _(pool):
            for r in range(2):
                pool.memset(u[r][:, 0:PAD], 0.0)
                pool.memset(run[r][:, 0:PAD], 0.0).then_inc(cleared, 1)
            pool.wait_ge(w_hi_ready, 1)
            pool.tensor_tensor(w_lo[:], w_raw[:], w_hi[:].bitcast(F32), ALU.subtract).then_inc(w_lo_ready, 1)
            for g in range(NGR):
                pool.wait_ge(hi_ready, g + 1)
                pool.tensor_tensor(d_lo[g % 2][:], diff[g % 2][:], d_hi[g % 2][:].bitcast(F32), ALU.subtract
                                   ).then_inc(lo_ready, 1)

        @block.vector
        def _(dve):
            steps = 0

            def chain(ins):
                nonlocal steps
                steps += 1
                ins.then_inc(chained, 1)
                dve.wait_ge(chained, steps)

            dve.wait_ge(cleared, 2)
            dve.wait_ge(consts, 32)
            for g, win in enumerate(WINDOWS):
                token = u[g % 2]
                dve.wait_ge(u_loaded[g % 2], 16 * (g // 2 + 1))
                src, span = token, 1
                for r in range(win.bit_length() - 1):
                    dst = run[r % 2]
                    chain(dve.tensor_tensor(dst[:, PAD:], src[:, PAD:], src[:, PAD - span:PAD + SEQ - span], ALU.add))
                    src, span = dst, 2 * span
                if g >= 2:
                    dve.wait_ge(lo_ready, g - 1)
                chain(dve.scalar_tensor_tensor(diff[g % 2][:], src[:, PAD:], 1.0 / win, token[:, PAD:],
                                               ALU.mult, ALU.subtract))
                chain(dve.tensor_tensor(diff[g % 2][:, 0:16], src[:, PAD:PAD + 16], edges[:, g, :], ALU.mult))
                dve.tensor_tensor(diff[g % 2][:, 0:16], diff[g % 2][:, 0:16], token[:, PAD:PAD + 16], ALU.subtract
                                  ).then_inc(differed, 1)

        @block.scalar
        def _(act):
            act.wait_ge(consts, 32)
            act.activation(w_hi[:], w_raw[:], ACT.Copy).then_inc(w_hi_ready, 1)

            def take(g):
                for s in range(NSB):
                    act.wait_ge(product, NSB * g + s + 1)
                    if g >= 1:
                        act.wait_ge(stored[s], 16 * g)
                    act.activation(stage[s][:], c.bank[4 * (g % 2) + s][:], ACT.Copy, scale=c.pool_scale[:, g:g + 1]
                                   ).then_inc(staged, 1)

            for g in range(NGR):
                act.wait_ge(differed, g + 1)
                if g >= 2:
                    act.wait_ge(product, NSB * (g - 1))
                act.activation(d_hi[g % 2][:], diff[g % 2][:], ACT.Copy).then_inc(hi_ready, 1)
                if g >= 1:
                    take(g - 1)
            take(NGR - 1)

        @block.tensor
        def _(pe):
            pe.wait_ge(w_lo_ready, 1)
            for g in range(NGR):
                pe.wait_ge(lo_ready, g + 1)
                for s in range(NSB):
                    if g >= 2:
                        pe.wait_ge(staged, NSB * (g - 2) + s + 1)
                    bank, tok = c.bank[4 * (g % 2) + s][:], slice(s * SB, (s + 1) * SB)
                    pe.matmul(bank, w_hi[:, g], d_hi[g % 2][:, tok], start=True, stop=False)
                    pe.matmul(bank, w_hi[:, g], d_lo[g % 2][:, tok], start=False, stop=False)
                    pe.matmul(bank, w_lo[:, g], d_hi[g % 2][:, tok], start=False, stop=True).then_inc(product, 1)


SD = 256
NSD = SEQ // SD


def output_projection(nc, c, name, w, y_in, x_in, gain_post, h_out, heads=None, gain_pre=None, hn_out=None):
    w_rows = w.rearrange("(k p) n -> k p n", p=P)
    x_tiles = x_in.rearrange("(t p) d -> t p d", p=P)
    h_tiles = h_out.rearrange("(t p) d -> t p d", p=P)
    HALF = KT // 2
    with ExitStack() as ctx:
        def sb(nm, shape, dt=F32):
            return ctx.enter_context(nc.sbuf_tensor(f"{name}_{nm}", shape, dt))

        def sem(nm):
            return c.semaphore(nc, ctx, (f"{name}_{nm}"))

        w_hi, w_lo = sb("w_hi", [P, KT, DM], F32R), sb("w_lo", [P, KT, DM], F32R)
        y = [sb(f"y{p}", [P, KT, SD]) for p in range(2)]
        y_hi = [sb(f"y_hi{p}", [P, KT, SD], F32R) for p in range(2)]
        y_lo = [sb(f"y_lo{p}", [P, KT, SD], F32R) for p in range(2)]
        g_post = sb("g_post", [P, DM])
        x = [sb(f"x{q}", [P, DM]) for q in range(2)]
        h = [sb(f"h{q}", [P, DM]) for q in range(2)]
        junk = sb("junk", [P, DM])
        ss = [sb(f"ss{q}", [P, 4]) for q in range(2)]
        ln = [sb(f"ln{q}", [P, 2]) for q in range(2)]
        rstd = [sb(f"rstd{q}", [P, 2]) for q in range(2)]
        if heads:
            gate = [sb(f"gate{p}", [P, KT, SD]) for p in range(2)]
            square, rms = sb("square", [P, HALF, SD]), sb("rms", [P, HALF, SD])
        if hn_out is not None:
            g_pre = sb("g_pre", [P, DM])
            xs = sb("xs", [P, DM])
            n_hi, n_lo = sb("n_hi", [P, KT, SD], F32R), sb("n_lo", [P, KT, SD], F32R)

        gains_loaded = sem("gains_loaded")
        w_loaded = [sem(f"w_loaded{q}") for q in range(2)]
        w_hi_ready, w_lo_ready = sem("w_hi_ready"), sem("w_lo_ready")
        y_loaded = [sem(f"y_loaded{p}") for p in range(2)]
        x_loaded = [sem(f"x_loaded{q}") for q in range(2)]
        squared, summed = sem("squared"), sem("summed")
        logged, rms_ready = sem("logged"), sem("rms_ready")
        normed, o_gated, b_gated = sem("normed"), sem("o_gated"), sem("b_gated")
        b_hi_ready, o_hi_ready = sem("b_hi_ready"), sem("o_hi_ready")
        b_lo_ready, o_lo_ready = sem("b_lo_ready"), sem("o_lo_ready")
        product = sem("product")
        sums, sum_ready, post_ln, post_ready = sem("sums"), sem("sum_ready"), sem("post_ln"), sem("post_ready")
        post_done = sem("post_done")
        h_ready = sem("h_ready")
        h_sum, pre_ln, pre_ready = sem("h_sum"), sem("pre_ln"), sem("pre_ready")
        xs_ready, turned, n_hi_ready, n_lo_ready = sem("xs_ready"), sem("turned"), sem("n_hi_ready"), sem("n_lo_ready")
        h_stored = [sem(f"h_stored{q}") for q in range(2)]
        n_stored = sem("n_stored")
        passed = sem("passed")
        block = ctx.enter_context(nc.Block())
        y_bank, t_bank, m_bank = c.bank[0:4], c.bank[4:6], c.bank[6:8]
        Y_LOADS = 16 * (3 if heads else 1)

        def walk(slot, drain):
            def run(i, eng_first, eng_last):
                for p in range(2):
                    for q in range(2):
                        back = 2 * p + q

                        def lacks(tiles_back=0, blocks_ahead=0):
                            return (eng_first and back < tiles_back) or (eng_last and p + blocks_ahead > 1)

                        slot(i, p, q, 4 * i + back, 2 * i + p, lacks)

            return run

        def passes(eng, slot, drain=None):
            run = walk(slot, drain)
            run(0, True, False)
            with eng.Fori(1, NSD // 2 - 1) as i:
                run(i, False, False)
            run(NSD // 2 - 1, False, True)
            if drain:
                drain()

        def flat(ap):
            return ap.rearrange("p f t -> p (f t)")

        o_rows, b_rows = slice(0, HALF), slice(HALF, KT)

        @block.sync
        def _(sp):
            sp.dma_start(g_post[:], bcast_row(gain_post, DM)).then_inc(gains_loaded, 16)
            if hn_out is not None:
                sp.dma_start(g_pre[:], bcast_row(gain_pre, DM)).then_inc(gains_loaded, 16)
                sp.sem_inc(n_stored, 32)
            for q in range(2):
                sp.sem_inc(h_stored[q], 16)

            def load_y(s, p):
                tok = bass.ds(s * SD, SD)
                if heads:
                    for dst, src in ((y[p][:, o_rows], heads[0]), (y[p][:, b_rows], heads[1]), (gate[p][:], y_in)):
                        sp.dma_start(dst, src[:, :, tok].rearrange("f p t -> p f t")).then_inc(y_loaded[p], 16)
                else:
                    sp.dma_start(y[p][:], y_in[:, :, tok].rearrange("f p t -> p f t")).then_inc(y_loaded[p], 16)

            def load_x(t, q):
                sp.dma_start(x[q][:], x_tiles[t]).then_inc(x_loaded[q], 16)

            for k in range(KT):
                if k >= 2:
                    sp.wait_ge(w_lo_ready, k - 1)
                sp.dma_start(h[k % 2][:], w_rows[k]).then_inc(w_loaded[k % 2], 16)
                if k == 1:
                    load_y(0, 0)
                    load_x(0, 0)
                    load_y(1, 1)
                    load_x(1, 1)

            def store_h(t, q):
                sp.wait_ge(h_ready, t + 1)
                sp.sem_inc(passed, 1)
                sp.dma_start(h_tiles[t], h[q][:]).then_inc(h_stored[q], 16)

            def store_n(s):
                sp.wait_ge(n_lo_ready, 2 * s + 2)
                sp.sem_inc(passed, 1)
                for half, n in ((0, n_hi), (1, n_lo)):
                    sp.dma_start(hn_out[half, s].bitcast(F32), n[:].bitcast(F32)).then_inc(n_stored, 16)

            def slot(i, p, q, t, s, lacks):
                if q == 0 and not lacks(blocks_ahead=2):
                    sp.wait_ge(o_lo_ready, s + 1)
                    sp.sem_inc(passed, 1)
                    sp.wait_ge(b_lo_ready, s + 1)
                    sp.sem_inc(passed, 1)
                    load_y(s + 2, p)
                if not lacks(tiles_back=1):
                    store_h(t - 1, 1 - q)
                    if not (lacks(blocks_ahead=1) and q == 1):
                        load_x(t + 1, 1 - q)
                if hn_out is not None and q == 1 and not lacks(tiles_back=3):
                    store_n(s - 1)

            def drain():
                store_h(TT - 1, 1)
                if hn_out is not None:
                    store_n(NSD - 1)
                    sp.wait_ge(n_stored, 32 * (NSD + 1))
                for q in range(2):
                    sp.wait_ge(h_stored[q], 16 * (TT // 2 + 1))

            passes(sp, slot, drain)

        @block.gpsimd
        def _(pool):
            for k in range(KT):
                pool.wait_ge(w_hi_ready, k + 1)
                pool.tensor_tensor(w_lo[:, k], h[k % 2][:], w_hi[:, k].bitcast(F32), ALU.subtract).then_inc(w_lo_ready, 1)

            def b_side(s, p, loads):
                if heads:
                    pool.wait_ge(y_loaded[p], Y_LOADS * loads)
                    pool.tensor_tensor(y[p][:, b_rows], y[p][:, b_rows], gate[p][:, b_rows], ALU.mult
                                       ).then_inc(b_gated, 1)

            def o_side(s, p):
                if heads:
                    pool.wait_ge(normed, s + 1)
                    pool.tensor_tensor(y[p][:, o_rows], y[p][:, o_rows], gate[p][:, o_rows], ALU.mult
                                       ).then_inc(o_gated, 1)
                pool.wait_ge(b_hi_ready, s + 1)
                pool.tensor_tensor(y_lo[p][:, b_rows], y[p][:, b_rows], y_hi[p][:, b_rows].bitcast(F32), ALU.subtract
                                   ).then_inc(b_lo_ready, 1)

            def residual(t, q, loads):
                pool.wait_ge(x_loaded[q], 16 * loads)
                pool.wait_ge(post_done, t + 1)
                pool.tensor_tensor(h[q][:], h[q][:], x[q][:], ALU.add).then_inc(h_ready, 1)

            b_side(0, 0, 1)
            o_side(0, 0)

            def slot(i, p, q, t, s, lacks):
                if not lacks(tiles_back=1):
                    residual(t - 1, 1 - q, 2 * i + p + (1 if q == 1 else 0))
                if not lacks(blocks_ahead=1):
                    if q == 0:
                        b_side(s + 1, 1 - p, i + 1 + p)
                    else:
                        o_side(s + 1, 1 - p)

            passes(pool, slot, lambda: residual(TT - 1, 1, TT // 2))

        @block.scalar
        def _(act):
            for k in range(KT):
                act.wait_ge(w_loaded[k % 2], 16 * (k // 2 + 1))
                act.activation(w_hi[:, k], h[k % 2][:], ACT.Copy).then_inc(w_hi_ready, 1)

            def squares(s, p, loads):
                if heads:
                    act.wait_ge(y_loaded[p], Y_LOADS * loads)
                    act.activation(square[:], y[p][:, o_rows], ACT.Square).then_inc(squared, 1)

            def rms_of_heads(s):
                if heads:
                    for m in range(2):
                        act.wait_ge(summed, 2 * s + m + 1)
                        act.activation(flat(rms[:])[:, m * SB:(m + 1) * SB], m_bank[m][:], ACT.Ln, bias=c.eps[:],
                                       scale=1.0 / P).then_inc(logged, 1)
                    act.wait_ge(logged, 2 * s + 2)
                    act.activation(rms[:], rms[:], ACT.Exp, scale=-0.5).then_inc(rms_ready, 1)

            def his(s, p, loads):
                if heads:
                    act.wait_ge(b_gated, s + 1)
                else:
                    act.wait_ge(y_loaded[p], Y_LOADS * loads)
                act.activation(y_hi[p][:, b_rows], y[p][:, b_rows], ACT.Copy).then_inc(b_hi_ready, 1)
                if heads:
                    act.wait_ge(o_gated, s + 1)
                act.activation(y_hi[p][:, o_rows], y[p][:, o_rows], ACT.Copy).then_inc(o_hi_ready, 1)

            def post(t, q):
                act.wait_ge(product, t + 1)
                for m in range(2):
                    act.activation(junk[:, m * SB:(m + 1) * SB], y_bank[2 * q + m][:], ACT.Square,
                                   accum_out=ss[q][:, m:m + 1]).then_inc(sums, 1)
                act.wait_ge(sum_ready, t + 1)
                act.activation(ln[q][:, 0:1], ss[q][:, 2:3], ACT.Ln, bias=c.eps[:], scale=1.0 / DM).then_inc(post_ln, 1)
                act.wait_ge(post_ln, t + 1)
                act.activation(rstd[q][:, 0:1], ln[q][:, 0:1], ACT.Exp, scale=-0.5).then_inc(post_ready, 1)

            def pre(t, q):
                if hn_out is not None:
                    act.wait_ge(h_ready, t + 1)
                    act.activation(junk[:], h[q][:], ACT.Square, accum_out=ss[q][:, 3:4]).then_inc(h_sum, 1)
                    act.wait_ge(h_sum, t + 1)
                    act.activation(ln[q][:, 1:2], ss[q][:, 3:4], ACT.Ln, bias=c.eps[:], scale=1.0 / DM).then_inc(pre_ln, 1)
                    act.wait_ge(pre_ln, t + 1)
                    act.activation(rstd[q][:, 1:2], ln[q][:, 1:2], ACT.Exp, scale=-0.5).then_inc(pre_ready, 1)

            def norm_hi(t, q, s):
                if hn_out is not None:
                    if q == 0:
                        act.wait_ge(n_stored, 32 * (s + 1))
                    act.wait_ge(turned, t + 1)
                    for m in range(2):
                        hi = act.activation(n_hi[:, 4 * m:4 * m + 4, q * P:(q + 1) * P],
                                            t_bank[m][:].rearrange("p (k n) -> p k n", k=4), ACT.Copy)
                    hi.then_inc(n_hi_ready, 1)

            squares(0, 0, 1)
            rms_of_heads(0)
            his(0, 0, 1)

            def slot(i, p, q, t, s, lacks):
                if not lacks(tiles_back=1):
                    post(t - 1, 1 - q)
                if not lacks(blocks_ahead=1):
                    if q == 0:
                        squares(s + 1, 1 - p, i + 1 + p)
                    else:
                        rms_of_heads(s + 1)
                if not lacks(tiles_back=2):
                    norm_hi(t - 2, q, s - 1)
                if not lacks(tiles_back=1):
                    pre(t - 1, 1 - q)
                if not lacks(blocks_ahead=1) and q == 1:
                    his(s + 1, 1 - p, i + 1 + p)

            def drain():
                post(TT - 1, 1)
                norm_hi(TT - 2, 0, NSD - 1)
                pre(TT - 1, 1)
                norm_hi(TT - 1, 1, NSD - 1)

            passes(act, slot, drain)

        @block.vector
        def _(dve):
            dve.wait_ge(gains_loaded, 32 if hn_out is not None else 16)

            def subln(s, p):
                if heads:
                    dve.wait_ge(rms_ready, s + 1)
                    dve.scalar_tensor_tensor(flat(y[p][:, o_rows]), flat(y[p][:, o_rows]), c.subln[:], flat(rms[:]),
                                             ALU.mult, ALU.mult).then_inc(normed, 1)

            def o_lo(s, p):
                dve.wait_ge(o_hi_ready, s + 1)
                dve.tensor_tensor(y_lo[p][:, o_rows], y[p][:, o_rows], y_hi[p][:, o_rows].bitcast(F32), ALU.subtract
                                  ).then_inc(o_lo_ready, 1)

            def post(t, q, stores):
                dve.wait_ge(sums, 2 * t + 2)
                dve.tensor_tensor(ss[q][:, 2:3], ss[q][:, 0:1], ss[q][:, 1:2], ALU.add).then_inc(sum_ready, 1)
                dve.wait_ge(h_stored[q], 16 * stores)
                dve.wait_ge(post_ready, t + 1)
                for m in range(2):
                    cols = slice(m * SB, (m + 1) * SB)
                    z = dve.scalar_tensor_tensor(h[q][:, cols], y_bank[2 * q + m][:], rstd[q][:, 0:1], g_post[:, cols],
                                                 ALU.mult, ALU.mult)
                z.then_inc(post_done, 1)

            def pre(t, q):
                if hn_out is not None:
                    dve.wait_ge(pre_ready, t + 1)
                    dve.scalar_tensor_tensor(xs[:], h[q][:], rstd[q][:, 1:2], g_pre[:], ALU.mult, ALU.mult
                                             ).then_inc(xs_ready, 1)

            def norm_lo(t, q):
                if hn_out is not None:
                    dve.wait_ge(n_hi_ready, t + 1)
                    for m in range(2):
                        where = (slice(None), slice(4 * m, 4 * m + 4), slice(q * P, (q + 1) * P))
                        lo = dve.tensor_tensor(n_lo[where], t_bank[m][:].rearrange("p (k n) -> p k n", k=4),
                                               n_hi[where].bitcast(F32), ALU.subtract)
                    lo.then_inc(n_lo_ready, 1)

            subln(0, 0)
            o_lo(0, 0)

            def slot(i, p, q, t, s, lacks):
                if not lacks(tiles_back=1):
                    post(t - 1, 1 - q, 2 * i + p + (1 if q == 1 else 0))
                if not lacks(blocks_ahead=1) and q == 1:
                    subln(s + 1, 1 - p)
                if not lacks(tiles_back=2):
                    norm_lo(t - 2, q)
                if not lacks(tiles_back=1):
                    pre(t - 1, 1 - q)
                if not lacks(blocks_ahead=1) and q == 1:
                    o_lo(s + 1, 1 - p)

            def drain():
                post(TT - 1, 1, TT // 2)
                norm_lo(TT - 2, 0)
                pre(TT - 1, 1)
                norm_lo(TT - 1, 1)

            passes(dve, slot, drain)

        @block.tensor
        def _(pe):
            def head_sums(s, ):
                if heads:
                    if not isinstance(s, int) or s > 0:
                        pe.wait_ge(logged, 2 * s)
                    pe.wait_ge(squared, s + 1)
                    for m in range(2):
                        pe.matmul(m_bank[m][:], c.ones[:], flat(square[:])[:, m * SB:(m + 1) * SB],
                                  start=True, stop=True).then_inc(summed, 1)

            def multiply(t, p, q, m):
                bank = y_bank[2 * q + m][:]
                tok, cols = slice(q * P, (q + 1) * P), slice(m * SB, (m + 1) * SB)
                for k in range(KT):
                    pe.matmul(bank, y_hi[p][:, k, tok], w_hi[:, k, cols], start=(k == 0), stop=False)
                    pe.matmul(bank, y_hi[p][:, k, tok], w_lo[:, k, cols], start=False, stop=False)
                    mm = pe.matmul(bank, y_lo[p][:, k, tok], w_hi[:, k, cols], start=False, stop=(k == KT - 1))
                if m == 1:
                    mm.then_inc(product, 1)

            def turn(t):
                if hn_out is not None:
                    if not isinstance(t, int) or t > 0:
                        pe.wait_ge(n_lo_ready, t)
                    pe.wait_ge(xs_ready, t + 1)
                    for k in range(KT):
                        tr = pe.transpose(t_bank[k // 4][:, (k % 4) * P:(k % 4 + 1) * P], xs[:, k * P:(k + 1) * P],
                                          c.ident[:])
                    tr.then_inc(turned, 1)

            head_sums(0)
            pe.wait_ge(w_lo_ready, KT)

            def slot(i, p, q, t, s, lacks):
                if q == 0:
                    pe.wait_ge(o_lo_ready, s + 1)
                    pe.wait_ge(b_lo_ready, s + 1)
                if not lacks(tiles_back=2):
                    pe.wait_ge(post_done, t - 1)
                multiply(t, p, q, 0)
                if not lacks(tiles_back=2):
                    turn(t - 2)
                multiply(t, p, q, 1)
                if q == 0 and not lacks(blocks_ahead=1):
                    head_sums(s + 1)

            def drain():
                turn(TT - 2)
                turn(TT - 1)

            passes(pe, slot, drain)


def sliding_window_attention(nc, c, proj, y_out):
    BT = 256
    BLOCKS = SEQ // BT
    PER = 8
    BATCHES = BLOCKS * PER
    UN = 4
    HEADS1 = 16
    KEEP = HD + BT
    PIECES = 4
    with ExitStack() as ctx:
        def sb(name, shape, dt=F32):
            return ctx.enter_context(nc.sbuf_tensor("sw_" + name, shape, dt))

        def sem(name):
            return c.semaphore(nc, ctx, ("sw_" + name))

        raw_q = [sb(f"raw_q{p}", [P, HEADS1, BT]) for p in range(2)]
        q_hi = [sb(f"q_hi{p}", [P, BT // HD, HEADS1, HD], F32R) for p in range(2)]
        q_lo = [sb(f"q_lo{p}", [P, BT // HD, HEADS1, HD], F32R) for p in range(2)]
        raw_k = [sb(f"raw_k{p}", [P, 2, KEEP]) for p in range(2)]
        k_take = sb("k_take", [P, 2, KEEP])
        k_stack = [sb(f"k_stack{p}", [P, 2, KEEP], F32R) for p in range(2)]
        raw_v = [sb(f"raw_v{p}", [P, KEEP]) for p in range(2)]
        v_hi = [sb(f"v_hi{p}", [P, 4, 2, 2, HD], F32R) for p in range(2)]
        v_lo = [sb(f"v_lo{p}", [P, 4, 2, 2, HD], F32R) for p in range(2)]
        gate = [sb(f"gate{p}", [P, KT, BT]) for p in range(2)]
        y = [sb(f"y{p}", [P, KT, BT]) for p in range(2)]
        probs = [sb(f"probs{r}", [P, UN, P]) for r in range(4)]
        wt_hi = [sb(f"wt_hi{r}", [P, UN * P], F32R) for r in range(2)]
        wt_lo = [sb(f"wt_lo{r}", [P, UN * P], F32R) for r in range(2)]
        neg_sink, sink = sb("neg_sink", [P, 2, UN]), sb("sink", [P, 2, UN])
        neg_max = [sb(f"neg_max{r}", [P, UN]) for r in range(4)]
        shift = [sb(f"shift{r}", [P, UN]) for r in range(4)]
        sums = [sb(f"sums{r}", [P, UN]) for r in range(4)]
        sink_exp = [sb(f"sink_exp{r}", [P, UN]) for r in range(4)]
        total = [sb(f"total{r}", [P, UN]) for r in range(4)]
        inverse = [sb(f"inverse{r}", [P, UN]) for r in range(4)]

        qkv_loaded = [sem(f"qkv_loaded{p}") for p in range(2)]
        gate_loaded = [sem(f"gate_loaded{p}") for p in range(2)]
        cleared, sinks_ready = sem("cleared"), sem("sinks_ready")
        q_hi_ready, q_lo_ready = sem("q_hi_ready"), sem("q_lo_ready")
        k_hi_ready, k_ready = sem("k_hi_ready"), sem("k_ready")
        v_turned, v_hi_ready, v_ready = sem("v_turned"), sem("v_hi_ready"), sem("v_ready")
        scores, maxed, floored, exped = sem("scores"), sem("maxed"), sem("floored"), sem("exped")
        totalled, inverted, weighted = sem("totalled"), sem("inverted"), sem("weighted")
        turned, turned_hi, turned_lo = sem("turned"), sem("turned_hi"), sem("turned_lo")
        product, gated = sem("product"), sem("gated")
        stored = [sem(f"stored{p}") for p in range(2)]
        passed, pool_passed = sem("passed"), sem("pool_passed")
        block = ctx.enter_context(nc.Block())
        s_bank, t_bank, o_bank, v_bank = c.bank[0:4], c.bank[4:6], c.bank[6], c.bank[7]
        QKV = 80

        def by_head(q, heads):
            return q[:, :, heads].rearrange("p c h t -> p h c t")

        def chunked(q, heads):
            return q[:, heads].rearrange("p h (c t) -> p h c t", t=HD)

        def passes(eng, slot, drain=None):
            def run(i, first, last):
                for p in range(2):
                    for j in range(PER):
                        def lacks(back=0, ahead=0):
                            return (first and PER * p + j < back) or (last and p + ahead > 1)

                        slot(i, p, j, 2 * PER * i + PER * p + j, lacks)

            run(0, True, False)
            with eng.Fori(1, BLOCKS // 2 - 1) as i:
                run(i, False, False)
            run(BLOCKS // 2 - 1, False, True)
            if drain:
                drain()

        def before(p, j, n):
            at = PER * p + j - n
            return (at // PER) % 2, at % PER

        @block.sync
        def _(sp):
            for p in range(2):
                sp.sem_inc(stored[p], 16)

            def load(B, p, first=False):
                skip = HD if first else 0
                tok = bass.ds(B * BT, BT)
                window = slice(0, BT) if first else bass.ds(B * BT - HD, KEEP)
                for half in range(2):
                    rows = slice(half * HD, (half + 1) * HD)
                    sp.dma_start(raw_q[p][rows], proj[0:KT].rearrange("g (m p) t -> p (g m) t", m=2)[:, :, tok]
                                 ).then_inc(qkv_loaded[p], 16)
                    sp.dma_start(raw_k[p][rows, :, skip:], proj[G1["k"]].rearrange("(m p) t -> p m t", m=2)[:, :, window]
                                 ).then_inc(qkv_loaded[p], 16)
                sp.dma_start(raw_v[p][:, skip:], proj[G1["v"]][:, window]).then_inc(qkv_loaded[p], 16)

            def load_gate(B, p):
                sp.dma_start(gate[p][:], proj[G1["gate"]:G1["gate"] + KT][:, :, bass.ds(B * BT, BT)]
                             .rearrange("g p t -> p g t")).then_inc(gate_loaded[p], 16)

            def store(B, p):
                sp.wait_ge(gated, PER * B + PER)
                sp.sem_inc(passed, 1)
                sp.dma_start(y_out[:, :, bass.ds(B * BT, BT)].rearrange("g p t -> p g t"), y[p][:]).then_inc(stored[p], 16)

            load(0, 0, first=True)
            load(1, 1)
            load_gate(0, 0)

            def slot(i, p, j, b, lacks):
                B = 2 * i + p
                if j == 0 and not lacks(ahead=2):
                    for ready, n in ((q_lo_ready, PIECES * (B + 1)), (k_ready, B + 1), (v_turned, B + 1)):
                        sp.wait_ge(ready, n)
                        sp.sem_inc(passed, 1)
                    load(B + 2, p)
                if j == 4 and not lacks(back=8):
                    store(B - 1, 1 - p)
                if j == 4 and not lacks(ahead=1):
                    load_gate(B + 1, 1 - p)

            def drain():
                store(BLOCKS - 1, 1)
                for p in range(2):
                    sp.wait_ge(stored[p], 16 * (BLOCKS // 2 + 1))

            passes(sp, slot, drain)

        @block.gpsimd
        def _(pool):
            pool.memset(raw_k[0][:, :, 0:HD], 0.0).then_inc(cleared, 1)
            pool.memset(raw_v[0][:, 0:HD], 0.0).then_inc(cleared, 1)

            def split_q(B, p, piece):
                heads = slice(4 * piece, 4 * piece + 4)
                pool.wait_ge(q_hi_ready, PIECES * B + piece + 1)
                pool.tensor_tensor(by_head(q_lo[p], heads), chunked(raw_q[p], heads),
                                   by_head(q_hi[p], heads).bitcast(F32), ALU.subtract
                                   ).then_inc(q_lo_ready, 1)

            def split_k(B, p):
                pool.wait_ge(k_hi_ready, B + 1)
                pool.tensor_tensor(k_stack[p][:], raw_k[p][:], k_take[:], ALU.subtract).then_inc(k_ready, 1)

            def normalize(b, r):
                pool.wait_ge(inverted, b + 1)
                pool.tensor_tensor(probs[r][:], probs[r][:], inverse[r][:].unsqueeze(2).to_broadcast([P, UN, P]),
                                   ALU.mult).then_inc(weighted, 1)

            for piece in range(PIECES):
                split_q(0, 0, piece)
            split_k(0, 0)

            def slot(i, p, j, b, lacks):
                if not lacks(back=1):
                    normalize(b - 1, (j - 1) % 4)
                if not lacks(ahead=1):
                    if 1 <= j <= PIECES:
                        split_q(2 * i + p + 1, 1 - p, j - 1)
                    if j == PIECES + 1:
                        split_k(2 * i + p + 1, 1 - p)

            passes(pool, slot, lambda: normalize(BATCHES - 1, 3))

        @block.scalar
        def _(act):
            def split_q(B, p, piece, loads):
                heads = slice(4 * piece, 4 * piece + 4)
                act.wait_ge(qkv_loaded[p], QKV * loads)
                act.activation(by_head(q_hi[p], heads), chunked(raw_q[p], heads), ACT.Copy).then_inc(q_hi_ready, 1)

            def split_k(B, p):
                act.activation(k_take[:].bitcast(F32R), raw_k[p][:], ACT.Copy, scale=c.lower[:]).then_inc(k_hi_ready, 1)

            def values_hi(B, p):
                act.wait_ge(v_turned, B + 1)
                act.activation(v_hi[p][:], v_bank[:].rearrange("p (w k d) -> p w k d", w=4, k=2).unsqueeze(3)
                               .to_broadcast([P, 4, 2, 2, HD]), ACT.Copy).then_inc(v_hi_ready, 1)

            def exponentials(b, p, j):
                r = j % 4
                act.wait_ge(floored, b + 1)
                for u in range(UN):
                    act.activation(probs[r][:, u], s_bank[r][:, u * P:(u + 1) * P], ACT.Exp, bias=neg_max[r][:, u:u + 1],
                                   accum_out=sums[r][:, u:u + 1])
                act.activation(sink_exp[r][:], shift[r][:], ACT.Exp).then_inc(exped, 1)

            def weights_hi(b, r):
                act.wait_ge(turned, b + 1)
                act.activation(wt_hi[r][:], t_bank[r][:], ACT.Copy).then_inc(turned_hi, 1)

            act.wait_ge(cleared, 2)
            for piece in range(PIECES):
                split_q(0, 0, piece, 1)
            split_k(0, 0)
            values_hi(0, 0)

            def slot(i, p, j, b, lacks):
                exponentials(b, p, j)
                if not lacks(back=2):
                    weights_hi(b - 2, j % 2)
                if not lacks(ahead=1):
                    B = 2 * i + p + 1
                    if 1 <= j <= PIECES:
                        split_q(B, 1 - p, j - 1, i + 1 + p)
                    if j == PIECES + 1:
                        split_k(B, 1 - p)
                        values_hi(B, 1 - p)

            def drain():
                weights_hi(BATCHES - 2, 0)
                weights_hi(BATCHES - 1, 1)

            passes(act, slot, drain)

        @block.vector
        def _(dve):
            for half in range(2):
                rows = slice(half * HD, (half + 1) * HD)
                dve.tensor_copy(sink[rows], c.sinks[rows].rearrange("p (k u m) -> p k u m", k=2, m=2)[:, :, :, half])
                dve.tensor_scalar(neg_sink[rows], c.sinks[rows].rearrange("p (k u m) -> p k u m", k=2, m=2)[:, :, :, half],
                                  -1.0, None, ALU.mult).then_inc(sinks_ready, 1)
            dve.wait_ge(sinks_ready, 2)

            def values_lo(B, p):
                dve.wait_ge(v_hi_ready, B + 1)
                windows = v_bank[:].rearrange("p (w k d) -> p w k d", w=4, k=2)
                for twice in range(2):
                    lo = dve.tensor_tensor(v_lo[p][:, :, :, twice], windows, v_hi[p][:, :, :, twice].bitcast(F32),
                                           ALU.subtract)
                lo.then_inc(v_ready, 1)

            def maxima(b, j):
                r, kv = j % 4, j % 2
                dve.wait_ge(scores, b + 1)
                dve.tensor_reduce(neg_max[r][:], s_bank[r][:].rearrange("p (u k) -> p u k", u=UN), AX.X, ALU.max,
                                  negate=True).then_inc(maxed, 1)
                dve.wait_ge(maxed, 2 * b + 1)
                dve.tensor_tensor(neg_max[r][:], neg_max[r][:], neg_sink[:, kv], ALU.min).then_inc(maxed, 1)
                dve.wait_ge(maxed, 2 * b + 2)
                dve.tensor_tensor(shift[r][:], sink[:, kv], neg_max[r][:], ALU.add).then_inc(floored, 1)

            def inverses(b, r):
                dve.wait_ge(exped, b + 1)
                dve.tensor_tensor(total[r][:], sums[r][:], sink_exp[r][:], ALU.add).then_inc(totalled, 1)
                dve.wait_ge(totalled, b + 1)
                dve.reciprocal(inverse[r][:], total[r][:]).then_inc(inverted, 1)

            def weights_lo(b, r):
                dve.wait_ge(turned_hi, b + 1)
                dve.tensor_tensor(wt_lo[r][:], t_bank[r][:], wt_hi[r][:].bitcast(F32), ALU.subtract).then_inc(turned_lo, 1)

            def take(b, p, j, B_loads, stores):
                kv, tok = j % 2, slice((j // 2) * HD, (j // 2 + 1) * HD)
                if j == 0:
                    dve.wait_ge(gate_loaded[p], 16 * B_loads)
                    dve.wait_ge(stored[p], 16 * B_loads)
                dve.wait_ge(product, b + 1)
                for half in range(2):
                    rows = slice(half * HD, (half + 1) * HD)
                    groups = slice(UN * kv, UN * kv + UN)
                    last = dve.tensor_tensor(y[p][rows, groups, tok],
                                             o_bank[rows].rearrange("p (u m q) -> p u m q", u=UN, m=2)[:, :, half],
                                             gate[p][rows, groups, tok], ALU.mult)
                last.then_inc(gated, 1)

            values_lo(0, 0)

            def slot(i, p, j, b, lacks):
                maxima(b, j)
                if not lacks(back=1):
                    inverses(b - 1, (j - 1) % 4)
                if not lacks(back=2):
                    weights_lo(b - 2, j % 2)
                if not lacks(back=3):
                    pb, jb = before(p, j, 3)
                    loads = i + 1 if not (p == 0 and j < 3) else i
                    take(b - 3, pb, jb, loads, None)
                if not lacks(ahead=1) and j == PIECES + 1:
                    values_lo(2 * i + p + 1, 1 - p)

            def drain():
                inverses(BATCHES - 1, 3)
                for b in (BATCHES - 2, BATCHES - 1):
                    weights_lo(b, b % 2)
                for b in (BATCHES - 3, BATCHES - 2, BATCHES - 1):
                    take(b, 1, b % PER, BLOCKS // 2, None)

            passes(dve, slot, drain)

        @block.tensor
        def _(pe):
            def turn_values(B, p, loads):
                if loads is not None:
                    pe.wait_ge(qkv_loaded[p], QKV * loads)
                if not isinstance(B, int) or B > 0:
                    pe.wait_ge(v_ready, B)
                for w in range(4):
                    tr = pe.transpose(v_bank[:, w * P:(w + 1) * P], raw_v[p][:, w * HD:w * HD + P], c.ident[:])
                tr.then_inc(v_turned, 1)

            def score(b, p, j, B, first, lacks):
                n, kv, r = j // 2, j % 2, j % 4
                if j == 0:
                    pe.wait_ge(q_lo_ready, PIECES * (B + 1))
                    pe.wait_ge(k_ready, B + 1)
                if not lacks(back=4):
                    pe.wait_ge(exped, b - 3)
                keys = k_stack[p][:, kv, n * HD:n * HD + P]
                for u in range(UN):
                    bank = s_bank[r][:, u * P:(u + 1) * P]
                    heads = slice(8 * kv + 2 * u, 8 * kv + 2 * u + 2)
                    pe.matmul(bank, q_hi[p][:, n, heads], keys, start=True, stop=False)
                    if first:
                        pe.matmul(bank[:, 0:HD], c.mask_all[:], c.mask_k[:], start=False, stop=False)
                    mm = pe.matmul(bank, q_lo[p][:, n, heads], keys, start=False, stop=True)
                mm.then_inc(scores, 1)

            def turn_weights(b, j, lacks):
                if not lacks(back=4):
                    pe.wait_ge(turned_lo, b - 1)
                pe.wait_ge(weighted, b + 1)
                for u in range(UN):
                    tr = pe.transpose(t_bank[j % 2][:, u * P:(u + 1) * P], probs[j % 4][:, u], c.ident[:])
                tr.then_inc(turned, 1)

            def values(b, p, j, lacks):
                n, kv, r = j // 2, j % 2, j % 2
                if not lacks(back=4):
                    pe.wait_ge(gated, b)
                pe.wait_ge(turned_lo, b + 1)
                pe.matmul(o_bank[:], v_hi[p][:, n, kv], wt_hi[r][:], start=True, stop=False)
                pe.matmul(o_bank[:], v_hi[p][:, n, kv], wt_lo[r][:], start=False, stop=False)
                pe.matmul(o_bank[:], v_lo[p][:, n, kv], wt_hi[r][:], start=False, stop=True).then_inc(product, 1)

            pe.wait_ge(cleared, 2)
            turn_values(0, 0, 1)

            def slot(i, p, j, b, lacks):
                B = 2 * i + p
                if j == 0:
                    pe.wait_ge(v_ready, B + 1)
                if j == PIECES and not lacks(ahead=1):
                    turn_values(B + 1, 1 - p, i + 1 + p)
                score(b, p, j, B, isinstance(b, int) and b < 2, lacks)
                if not lacks(back=2):
                    turn_weights(b - 2, (j - 2) % PER, lacks)
                if not lacks(back=3):
                    pb, jb = before(p, j, 3)
                    values(b - 3, pb, jb, lacks)

            def drain():
                none = lambda back=0, ahead=0: False
                turn_weights(BATCHES - 2, 6, none)
                values(BATCHES - 3, 1, 5, none)
                turn_weights(BATCHES - 1, 7, none)
                values(BATCHES - 2, 1, 6, none)
                values(BATCHES - 1, 1, 7, none)

            passes(pe, slot, drain)


def build(nc, a, out):
    def dram(name, shape, dt=F32):
        return nc.dram_tensor(name, shape, dt).ap()

    proj0, proj1 = dram("proj0", (NG0, P, SEQ)), dram("proj1", (NG1, P, SEQ))
    heads0, pooled0 = dram("heads0", (4, P, SEQ)), dram("pooled0", (4, P, SEQ))
    h1 = dram("h1", (SEQ, DM))
    hn1 = dram("hn1", (2, NSD, P, KT, SD), F32R)
    y1 = dram("y1", (KT, P, SEQ))
    c = Core()
    c.rope_cos, c.rope_sin = a["rope_cos"], a["rope_sin"]
    with ExitStack() as ctx:
        def sb(name, shape, dt=F32):
            return ctx.enter_context(nc.sbuf_tensor(name, shape, dt))

        c.bank = [ctx.enter_context(nc.psum_tensor(f"bank{i}", [P, SB], F32)) for i in range(8)]
        c.ident, c.ones, c.eps = sb("ident", [P, P]), sb("ones", [P, P]), sb("eps", [P, 1])
        c.lam, c.subln, c.lower = sb("lam", [P, 2]), sb("subln", [P, 1]), sb("lower", [P, 1])
        c.pool_scale, c.sinks = sb("pool_scale", [P, len(WINDOWS)]), sb("sinks", [P, 16])
        c.mask_q, c.mask_all, c.mask_k = sb("mask_q", [P, P], F32R), sb("mask_all", [P, P], F32R), sb("mask_k", [P, HD], F32R)

        phase_constants(nc, c, a)
        with ExitStack() as layer:
            hn_hi = layer.enter_context(nc.sbuf_tensor("hn0_hi", [P, KT, SEQ], F32R))
            hn_lo = layer.enter_context(nc.sbuf_tensor("hn0_lo", [P, KT, SEQ], F32R))
            norm_and_transpose(nc, c, a["x"][0], a["norm_pre"][0], hn_hi, hn_lo)
            in_projection(nc, "in0", c, a["ab_w_in"][0], hn_hi, hn_lo, PARTS0, proj0)
        differential_attention(nc, c, proj0, heads0)
        pooling(nc, c, proj0, a["pool_w"][0], a["pool_edge"], pooled0)
        output_projection(nc, c, "out0", a["ab_w_out"][0], proj0[G0["gate"]:G0["gate"] + KT], a["x"][0],
                          a["norm_post"][0], h1, heads=(heads0, pooled0), gain_pre=a["norm_pre"][1], hn_out=hn1)
        c.clear_spent(nc)
        with ExitStack() as layer:
            hn_hi = layer.enter_context(nc.sbuf_tensor("hn1_hi", [P, KT, SEQ], F32R))
            hn_lo = layer.enter_context(nc.sbuf_tensor("hn1_lo", [P, KT, SEQ], F32R))
            in_projection(nc, "in1", c, a["c_w_in"][0], hn_hi, hn_lo, PARTS1, proj1, load=(hn1[0], hn1[1]))
        sliding_window_attention(nc, c, proj1, y1)
        output_projection(nc, c, "out1", a["c_w_out"][0], y1, h1, a["norm_post"][1], out[0])


_INS = ["x", "norm_pre", "norm_post", "ab_w_in", "ab_w_out", "diff_lambda", "diff_subln",
        "pool_w", "pool_scale", "c_w_in", "c_w_out", "c_sinks"]


def kernel(**inputs):
    import concourse.bacc as bacc
    from concourse.bass_utils import run_bass_kernel_spmd as run

    nc = bacc.Bacc("TRN2", target_bir_lowering=False, num_devices=1)
    arrays = {name: np.ascontiguousarray(inputs[name]) for name in _INS}
    arrays["rope_cos"], arrays["rope_sin"] = rope_tables()
    arrays["pool_edge"] = pool_edge()
    arrays = {f"in_{name}": array for name, array in arrays.items()}
    args = {name[3:]: nc.dram_tensor(name, array.shape, mybir.dt.from_np(array.dtype), kind="ExternalInput").ap()
            for name, array in arrays.items()}
    out = nc.dram_tensor("out_0", (1, SEQ, DM), F32, kind="ExternalOutput").ap()
    build(nc, args, out)
    result = run(nc, [arrays], core_ids=[0])
    return result.results[0]["out_0"]
```

```python
from contextlib import ExitStack

import numpy as np

import concourse.bass as bass
from concourse import mybir

F32 = mybir.dt.float32
F32R = mybir.dt.float32r
ALU = mybir.AluOpType
ACT = mybir.ActivationFunctionType
AX = mybir.AxisListType

P = 128
SEQ = 2048
DM = 1024
KT = DM // P
TT = SEQ // P
SB = 512
NSB = SEQ // SB
EPS = 1e-6
ROPE_THETA = 10000.0

HEADS0 = 4
HD = 64
QK0, V0, U0 = 512, 512, 512
G0 = {"q": 0, "k": 4, "v": 8, "u": 12, "gate": 16}
G1 = {"q": 0, "k": 8, "v": 9, "gate": 10}
NG0, NG1 = 24, 18
WINDOWS = (2, 4, 8, 16)
LAMBDA_INIT = 0.2

PARTS0 = [(1, "query", "query"), (1, "query", "query"), (2, "rope", "rope"), (4, "plain", "plain"), (4, "silu", "silu")]
PARTS1 = [(4, "query", "query"), (1, "rope", "plain"), (4, "silu", "silu")]


def rope_tables():
    inv = (ROPE_THETA ** (-np.arange(0, HD, 2) / HD)).astype(np.float32)
    ang = np.arange(SEQ, dtype=np.float32)[None, :] * inv[:, None]
    cos, sin = np.cos(ang), np.sin(ang)
    return (np.ascontiguousarray(np.concatenate([cos, cos, cos, cos])),
            np.ascontiguousarray(np.concatenate([sin, -sin, sin, -sin])))


def pool_edge():
    t = np.zeros((P, len(WINDOWS), 16), np.float32)
    for g, w in enumerate(WINDOWS):
        t[:, g, :] = (np.float32(1.0) / np.minimum(np.arange(1, 17), w).astype(np.float32))[None, :]
    return t


class Core:

    def __init__(self):
        self.spent = []

    def semaphore(self, nc, ctx, name):
        made = ctx.enter_context(nc.semaphore(name))
        self.spent.append(made)
        return made

    def clear_spent(self, nc):
        with nc.Block() as block:
            @block.gpsimd
            def _(pool):
                for made in self.spent[0::3]:
                    pool.sem_clear(made)

            @block.vector
            def _(dve):
                for made in self.spent[1::3]:
                    dve.sem_clear(made)

            @block.scalar
            def _(act):
                for made in self.spent[2::3]:
                    act.sem_clear(made)
        self.spent = []


def bcast_row(vec, n):
    return vec.rearrange("(a n) -> a n", a=1).to_broadcast([P, n])


def phase_constants(nc, c, a):
    with ExitStack() as ctx:
        lam_in = ctx.enter_context(nc.sbuf_tensor("lam_in", [P, 4, HD], F32))
        lam_prod = ctx.enter_context(nc.sbuf_tensor("lam_prod", [P, 2, HD], F32))
        lam_sum = ctx.enter_context(nc.sbuf_tensor("lam_sum", [P, 2], F32))
        lam_exp = ctx.enter_context(nc.sbuf_tensor("lam_exp", [P, 2], F32))
        subln_in = ctx.enter_context(nc.sbuf_tensor("subln_in", [P, 1], F32))
        loaded = c.semaphore(nc, ctx, ("const_loaded"))
        zeroed = c.semaphore(nc, ctx, ("const_zeroed"))
        step = c.semaphore(nc, ctx, ("const_step"))
        exped = c.semaphore(nc, ctx, ("const_exped"))
        block = ctx.enter_context(nc.Block())

        @block.sync
        def _(sp):
            sp.dma_start(lam_in[:], a["diff_lambda"].rearrange("a n d -> a (n d)").to_broadcast([P, 4 * HD])
                         ).then_inc(loaded, 16)
            sp.dma_start(subln_in[:], a["diff_subln"].rearrange("a p -> p a")).then_inc(loaded, 16)
            sp.dma_start(c.pool_scale[:], a["pool_scale"].rearrange("a (g p) -> p (a g)", p=P),
                         allow_slow_non_contiguous=True).then_inc(loaded, 16)
            sp.dma_start(c.sinks[:], a["c_sinks"].to_broadcast([P, 16])).then_inc(loaded, 16)
            sp.wait_ge(loaded, 64)

        @block.gpsimd
        def _(pool):
            pool.memset(c.ident[:], 0.0).then_inc(zeroed, 1)
            pool.memset(c.ones[:], 1.0)
            pool.memset(c.eps[:], EPS)
            pool.memset(c.mask_q[:].bitcast(F32), 0.0).then_inc(zeroed, 1)
            pool.memset(c.mask_k[:].bitcast(F32), 0.0).then_inc(zeroed, 1)
            pool.memset(c.mask_all[:].bitcast(F32), 0.0).then_inc(zeroed, 1)
            pool.wait_ge(zeroed, 4)
            pool.memset(c.mask_q[0:1, 0:HD].bitcast(F32), 1.0)
            pool.memset(c.mask_all[0:1, :].bitcast(F32), 1.0)
            pool.memset(c.mask_k[0:1, :].bitcast(F32), -2.0 ** 120)
            pool.affine_select(out=c.ident[:], in_=c.ident[:], compare_op=ALU.not_equal, fill=1.0, base=0,
                               pattern=[[-1, P]], channel_multiplier=1).then_inc(zeroed, 1)

        @block.vector
        def _(dve):
            dve.memset(c.lower[0:HD, :], 0.0)
            dve.memset(c.lower[HD:P, :], 1.0)
            dve.wait_ge(loaded, 64)
            dve.tensor_tensor(lam_prod[:], lam_in[:, 0:4:2], lam_in[:, 1:4:2], ALU.mult).then_inc(step, 1)
            dve.wait_ge(step, 1)
            dve.reduce_sum(lam_sum[:], lam_prod[:], AX.X).then_inc(step, 1)
            dve.tensor_scalar(c.subln[:], subln_in[:], 1.0 - LAMBDA_INIT, None, ALU.mult)
            dve.memset(c.lam[:, 0:1], 1.0)
            dve.wait_ge(exped, 1)
            dve.scalar_tensor_tensor(c.lam[:, 1:2], lam_exp[:, 1:2], LAMBDA_INIT, lam_exp[:, 0:1],
                                     ALU.subtract, ALU.subtract).then_inc(step, 1)
            dve.wait_ge(step, 3)

        @block.scalar
        def _(act):
            act.wait_ge(step, 2)
            act.activation(lam_exp[:], lam_sum[:], ACT.Exp).then_inc(exped, 1)


def in_projection(nc, name, c, w, hn_hi, hn_lo, parts, out, load=None, norm=None):
    NX = 4
    SIDE = SB // P
    groups = sum(2 * n for n, _, _ in parts)
    w_groups = w.rearrange("(k p) n -> p k n", p=P)
    with ExitStack() as ctx:
        def sb(nm, shape, dt=F32):
            return ctx.enter_context(nc.sbuf_tensor(f"{name}_{nm}", shape, dt))

        def sem(nm):
            return c.semaphore(nc, ctx, (f"{name}_{nm}"))

        cos, sin = sb("cos", [P, SEQ]), sb("sin", [P, SEQ])
        w_raw = [sb(f"w_raw{b}", [P, KT, P]) for b in range(2)]
        w_hi = [sb(f"w_hi{b}", [P, KT, P], F32R) for b in range(2)]
        w_lo = [sb(f"w_lo{b}", [P, KT, P], F32R) for b in range(2)]
        stage = [sb(f"stage{s}", [P, SB]) for s in range(NSB)]
        direct = [sb(f"direct{r}", [P, SB]) for r in range(2)]
        rotated = [sb(f"rotated{r}", [P, SB]) for r in range(2)]
        if norm:
            x_tiles = norm[0].rearrange("(t p) d -> t p d", p=P)
            x = [sb(f"x{r}", [P, DM]) for r in range(NX)]
            gain = sb("gain", [P, DM])
            ss, ln, rstd = sb("ss", [P, TT]), sb("ln", [P, TT]), sb("rstd", [P, TT])
            x_loaded = [sem(f"x_loaded{r}") for r in range(NX)]
            gain_loaded, stat, rstd_ready = sem("gain_loaded"), sem("stat"), sem("rstd_ready")
            scaled, turned, tile_hi, tile_lo = sem("scaled"), sem("turned"), sem("tile_hi"), sem("tile_lo")

            def side_bank(t, h):
                return c.bank[4 + 2 * (t % 2) + h][:]

            def hn_cols(t, h):
                return slice(None), slice(4 * h, 4 * h + 4), slice(t * P, (t + 1) * P)

        def halves(s):
            return [slice(at, at + SB // 2) for at in (s * SB, s * SB + SB // 2)]

        tables = sem("tables_loaded")
        hn_loaded = [sem(f"hn_loaded{s}") for s in range(NSB)]
        hn_hi_ready = [sem(f"hn_hi_ready{s}") for s in range(NSB)]
        hn_split = [sem(f"hn_split{s}") for s in range(NSB)]
        w_loaded = [sem(f"w_loaded{b}") for b in range(2)]
        hi_ready = [sem(f"w_hi_ready{b}") for b in range(2)]
        lo_ready = [sem(f"w_lo_ready{b}") for b in range(2)]
        product = [sem(f"product{b}") for b in range(2)]
        bank_free = [sem(f"bank_free{b}") for b in range(2)]
        roped = sem("roped")
        stored = [sem(f"stored{s}") for s in range(NSB)]
        block = ctx.enter_context(nc.Block())

        def walk(eng, step, first=0):
            done, ropes = 0, 0
            for at, (pairs, even, odd) in enumerate(parts):
                looped = pairs - 1 if at == len(parts) - 1 else pairs
                turned = [kind in ("query", "rope") for kind in (even, odd)]
                per = sum(turned)

                def pair(i, last):
                    for b, kind in enumerate((even, odd)):
                        m = done // 2 + i
                        r = ropes + per * i + (b if turned[0] else 0)
                        step(2 * m + b, m, b, r, kind, last)

                if looped == 1:
                    pair(0, False)
                else:
                    with eng.Fori(0, looped) as i:
                        pair(i, False)
                if looped < pairs:
                    pair(looped, True)
                done += 2 * pairs
                ropes += per * pairs

        @block.sync
        def _(sp):
            for s in range(NSB):
                sp.sem_inc(stored[s], 16)

            def load_w(n, b):
                sp.dma_start(w_raw[b][:], w_groups[:, :, bass.ds(n * P, P)]).then_inc(w_loaded[b], 16)

            def load_x(t):
                sp.dma_start(x[t % NX][:], x_tiles[t]).then_inc(x_loaded[t % NX], 16)

            if norm:
                load_x(0)
                sp.dma_start(gain[:], bcast_row(norm[1], DM)).then_inc(gain_loaded, 16)
                load_x(1)
                for t in range(2, NX):
                    load_x(t)
            if load is None:
                load_w(0, 0)
                load_w(1, 1)
            else:
                for s in range(NSB):
                    for half in range(SB // SD):
                        tok = slice(s * SB + half * SD, s * SB + (half + 1) * SD)
                        sp.dma_start(hn_lo[:, :, tok].bitcast(F32), load[s * SB // SD + half]
                                     ).then_inc(hn_loaded[s], 16)
                    if s == 0:
                        load_w(0, 0)
                        load_w(1, 1)
            for t in range(NX, TT if norm else 0):
                sp.wait_ge(turned, t - NX + 1)
                load_x(t)
                if t == NX:
                    sp.dma_start(cos[:], c.rope_cos).then_inc(tables, 16)
                    sp.dma_start(sin[:], c.rope_sin).then_inc(tables, 16)
            if not norm:
                sp.dma_start(cos[:], c.rope_cos).then_inc(tables, 16)
                sp.dma_start(sin[:], c.rope_sin).then_inc(tables, 16)

            def step(n, m, b, r, kind, last):
                if not last:
                    sp.wait_ge(lo_ready[b], m + 1)
                    load_w(n + 2, b)
                for s in range(NSB):
                    if kind in ("query", "rope"):
                        sp.wait_ge(roped, 4 * r + s + 3)
                    else:
                        sp.wait_ge(bank_free[b], 4 * m + s + 5)
                    sp.dma_start(out[n, :, s * SB:(s + 1) * SB], stage[s][:]).then_inc(stored[s], 16)

            walk(sp, step)
            for s in range(NSB):
                sp.wait_ge(stored[s], 16 * (groups + 1))

        @block.scalar
        def _(act):
            for b in range(2):
                act.sem_inc(bank_free[b], NSB)

            def split(m, b):
                act.wait_ge(w_loaded[b], 16 * (m + 1))
                act.activation(w_hi[b][:], w_raw[b][:], ACT.Copy).then_inc(hi_ready[b], 1)

            def square(t):
                act.wait_ge(x_loaded[t % NX], 16 * (t // NX + 1))
                act.activation(hn_lo[:, :, (TT - 1) * P:], x[t % NX][:].rearrange("p (k n) -> p k n", n=P),
                               ACT.Square, accum_out=ss[:, t:t + 1]).then_inc(stat, 1)

            def logarithm(t):
                act.wait_ge(stat, 2 * t + 1)
                act.activation(ln[:, t:t + 1], ss[:, t:t + 1], ACT.Ln, bias=c.eps[:], scale=1.0 / DM).then_inc(stat, 1)

            def reciprocal_root(t):
                act.wait_ge(stat, 2 * t + 2)
                act.activation(rstd[:, t:t + 1], ln[:, t:t + 1], ACT.Exp, scale=-0.5).then_inc(rstd_ready, 1)

            def side_hi(t, h):
                if h == 0:
                    act.wait_ge(turned, t + 1)
                hi = act.activation(hn_hi[hn_cols(t, h)], side_bank(t, h).rearrange("p (k n) -> p k n", k=4), ACT.Copy)
                if h == 1:
                    hi.then_inc(tile_hi, 1)

            if norm:
                act.preload_act_table_set("natural_log_exp_and_others")
                for t in range(-2, TT):
                    if t + 2 < TT:
                        square(t + 2)
                    if t >= 0:
                        side_hi(t, 0)
                    if t + 2 < TT:
                        logarithm(t + 2)
                    if t >= 0:
                        side_hi(t, 1)
                    if t + 2 < TT:
                        reciprocal_root(t + 2)
                    if t in (0, 1):
                        split(0, t)
            act.preload_act_table_set("silu_and_others")
            if load is not None:
                for s in range(NSB):
                    act.wait_ge(hn_loaded[s], 16 * SB // SD)
                    for tok in halves(s):
                        act.activation(hn_hi[:, :, tok], hn_lo[:, :, tok].bitcast(F32), ACT.Copy
                                       ).then_inc(hn_hi_ready[s], 1)
                    if s == 0:
                        split(0, 0)
                        split(0, 1)

            def step(n, m, b, r, kind, last):
                for s in range(NSB):
                    if kind not in ("query", "rope"):
                        act.wait_ge(product[b], 4 * m + s + 1)
                        act.wait_ge(stored[s], 16 * (n + 1))
                        act.activation(stage[s][:], c.bank[4 * b + s][:],
                                       ACT.Silu if kind == "silu" else ACT.Copy).then_inc(bank_free[b], 1)
                if not last:
                    act.wait_ge(product[b], 4 * m + 4)
                    split(m + 1, b)

            walk(act, step)

        @block.gpsimd
        def _(pool):
            pool.sem_inc(roped, 2)

            def split(m, b):
                pool.wait_ge(hi_ready[b], m + 1)
                pool.tensor_tensor(w_lo[b][:], w_raw[b][:], w_hi[b][:].bitcast(F32), ALU.subtract
                                   ).then_inc(lo_ready[b], 1)

            split(0, 0)
            split(0, 1)

            def step(n, m, b, r, kind, last):
                if kind in ("query", "rope"):
                    for s in range(NSB):
                        pool.wait_ge(bank_free[b], 4 * m + s + 5)
                        pool.wait_ge(stored[s], 16 * (n + 1))
                        pool.tensor_tensor(stage[s][:], direct[s % 2][:], rotated[s % 2][:], ALU.add
                                           ).then_inc(roped, 1)
                if not last:
                    split(m + 1, b)

            walk(pool, step)

        @block.vector
        def _(dve):
            if load is not None:
                for s in range(NSB):
                    for n, tok in enumerate(halves(s)):
                        dve.wait_ge(hn_hi_ready[s], n + 1)
                        dve.tensor_tensor(hn_lo[:, :, tok], hn_lo[:, :, tok].bitcast(F32), hn_hi[:, :, tok].bitcast(F32),
                                          ALU.subtract).then_inc(hn_split[s], 1)

            def scale(t):
                dve.wait_ge(rstd_ready, t + 1)
                dve.scalar_tensor_tensor(x[t % NX][:], x[t % NX][:], rstd[:, t:t + 1], gain[:], ALU.mult, ALU.mult
                                         ).then_inc(scaled, 1)

            def side_lo(t):
                dve.wait_ge(tile_hi, t + 1)
                for h in range(2):
                    lo = dve.tensor_tensor(hn_lo[hn_cols(t, h)], side_bank(t, h).rearrange("p (k n) -> p k n", k=4),
                                           hn_hi[hn_cols(t, h)].bitcast(F32), ALU.subtract)
                lo.then_inc(tile_lo, 1)

            if norm:
                dve.wait_ge(gain_loaded, 16)
                scale(0)
                scale(1)
            else:
                dve.wait_ge(tables, 32)

            def step(n, m, b, r, kind, last):
                if kind not in ("query", "rope"):
                    return
                first = norm is not None and isinstance(n, int) and n == 0
                if first:
                    for t in range(SIDE):
                        scale(t + 2)
                        side_lo(t)
                for s in range(NSB):
                    if first:
                        for t in range(SIDE * (s + 1), min(SIDE * (s + 2), TT)):
                            if t + 2 < TT:
                                scale(t + 2)
                            side_lo(t)
                        if s == 0:
                            dve.wait_ge(tables, 32)
                    dve.wait_ge(product[b], 4 * m + s + 1)
                    dve.wait_ge(roped, 4 * r + s + 1)
                    bank = c.bank[4 * b + s]
                    tok = slice(s * SB, (s + 1) * SB)
                    factor = HD ** -0.5 if kind == "query" else 1.0
                    dve.scalar_tensor_tensor(direct[s % 2][:], bank[:], factor, cos[:, tok], ALU.mult, ALU.mult)
                    for src, dst in ((0, 32), (32, 0), (64, 96), (96, 64)):
                        rot = dve.scalar_tensor_tensor(rotated[s % 2][dst:dst + 32, :], bank[src:src + 32, :], factor,
                                                       sin[src:src + 32, tok], ALU.mult, ALU.mult)
                    rot.then_inc(bank_free[b], 1)

            walk(dve, step)

        @block.tensor
        def _(pe):
            def turn(t):
                pe.wait_ge(scaled, t + 1)
                if t >= 2:
                    pe.wait_ge(tile_lo, t - 1)
                for k in range(KT):
                    tr = pe.transpose(side_bank(t, k // 4)[:, (k % 4) * P:(k % 4 + 1) * P],
                                      x[t % NX][:, k * P:(k + 1) * P], c.ident[:])
                tr.then_inc(turned, 1)

            if norm:
                for t in range(SIDE + 2):
                    turn(t)

            def step(n, m, b, r, kind, last):
                first = norm is not None and isinstance(n, int) and n == 0
                pe.wait_ge(lo_ready[b], m + 1)
                for s in range(NSB):
                    if first:
                        pe.wait_ge(tile_lo, SIDE * (s + 1))
                    if load is not None:
                        pe.wait_ge(hn_split[s], 2)
                    pe.wait_ge(bank_free[b], 4 * m + s + 1)
                    tok = slice(s * SB, (s + 1) * SB)
                    for k in range(KT):
                        bank = c.bank[4 * b + s][:]
                        pe.matmul(bank, w_hi[b][:, k], hn_hi[:, k, tok], start=(k == 0), stop=False)
                        pe.matmul(bank, w_hi[b][:, k], hn_lo[:, k, tok], start=False, stop=False)
                        mm = pe.matmul(bank, w_lo[b][:, k], hn_hi[:, k, tok], start=False, stop=(k == KT - 1))
                    mm.then_inc(product[b], 1)
                    if first:
                        for t in range(SIDE * (s + 1) + 2, min(SIDE * (s + 2) + 2, TT)):
                            turn(t)

            walk(pe, step)


def differential_attention(nc, c, proj, o_out):
    CH = 512
    STEPS = 2 * TT // 2
    UNITS = 2 * TT

    def chunks(u):
        keys = (u % TT + 1) * P
        return [(at, min(CH, keys - at)) for at in range(0, keys, CH)]

    chunk_base = [sum(len(chunks(v)) for v in range(u)) for u in range(UNITS + 1)]
    CHUNKS = chunk_base[UNITS]
    every = [(u, n) for u in range(UNITS) for n in range(len(chunks(u)))]
    by_vector = [(u, n) for u, n in every if len(chunks(u)) > 2 and n % 2 == 1]
    by_pool = [chunk for chunk in every if chunk not in by_vector]
    turn_of, turns = {}, 0
    turn_of["v", 0] = turns
    turns += 1
    for u in range(UNITS + 2):
        if u >= 2:
            for n in range(len(chunks(u - 2))):
                turn_of[u - 2, n] = turns
                turns += 1
        if u % 2 == 1 and u // 2 + 1 < STEPS:
            turn_of["v", u // 2 + 1] = turns
            turns += 1

    with ExitStack() as ctx:
        def sb(name, shape, dt=F32):
            return ctx.enter_context(nc.sbuf_tensor("da_" + name, shape, dt))

        def sem(name):
            return c.semaphore(nc, ctx, ("da_" + name))

        raw_k = [sb(f"raw_k{r}", [P, 2, 2 * P]) for r in range(2)]
        raw_q = [sb(f"raw_q{r}", [P, 2, 2 * P]) for r in range(2)]
        raw_v = [sb(f"raw_v{r}", [P, 2 * P]) for r in range(2)]
        k_stack = [sb(f"k_stack{h}", [P, 2, SEQ], F32R) for h in range(2)]
        k_take = [sb(f"k_take{r}", [P, 2, 2 * P]) for r in range(2)]
        q_hi = [sb(f"q_hi{r}", [P, 2, 2 * P], F32R) for r in range(2)]
        q_lo = [sb(f"q_lo{r}", [P, 2, 2 * P], F32R) for r in range(2)]
        v_hi = [sb(f"v_hi{h}", [P, TT, P], F32R) for h in range(2)]
        v_lo = [sb(f"v_lo{h}", [P, TT, P], F32R) for h in range(2)]
        probs = [sb(f"probs{r}", [P, 2, SEQ]) for r in range(3)]
        wt_hi = [sb(f"wt_hi{r}", [P, TT, 2 * P], F32R) for r in range(2)]
        wt_lo = [sb(f"wt_lo{r}", [P, TT, 2 * P], F32R) for r in range(2)]
        o_stage = [sb(f"o_stage{r}", [P, 2 * P]) for r in range(2)]
        neg_max = [sb(f"neg_max{r}", [P, 2, 4]) for r in range(2)]
        sums = [sb(f"sums{r}", [P, 2, 4]) for r in range(2)]
        least = [sb(f"least{r}", [P, 2]) for r in range(2)]
        shift = [sb(f"shift{r}", [P, 2, 4]) for r in range(2)]
        factor = [sb(f"factor{r}", [P, 2, 4]) for r in range(2)]
        part = [sb(f"part{r}", [P, 2, 4]) for r in range(2)]
        total = [sb(f"total{r}", [P, 2]) for r in range(2)]
        inverse = [sb(f"inverse{r}", [P, 2]) for r in range(2)]
        weight = [sb(f"weight{r}", [P, 2, 4]) for r in range(2)]

        raw_loaded = [sem(f"raw_loaded{r}") for r in range(2)]
        split_hi = sem("split_hi")
        split_lo = sem("split_lo")
        scores = sem("scores")
        maxed = sem("maxed")
        exped = sem("exped")
        shifted = sem("shifted")
        factored = sem("factored")
        stat = sem("stat")
        weighted = sem("weighted")
        second = sem("second")
        both_scaled = sem("both_scaled")
        pool_joined = sem("pool_joined")
        joined = sem("joined")
        turned = sem("turned")
        turned_hi = sem("turned_hi")
        turned_lo = sem("turned_lo")
        output = sem("output")
        staged = sem("staged")
        stored = [sem(f"stored{r}") for r in range(2)]
        sp_passed, pool_passed = sem("sp_passed"), sem("pool_passed")
        block = ctx.enter_context(nc.Block())
        s_bank, t_bank, o_bank = c.bank[0:4], c.bank[4:6], c.bank[6:8]
        LOADS = 80

        STATS = sum(3 if len(chunks(u)) > 1 else 1 for u in range(UNITS))
        stat_base = [sum(3 if len(chunks(v)) > 1 else 1 for v in range(u)) for u in range(UNITS + 1)]
        long_units = [u for u in range(UNITS) if len(chunks(u)) > 1]

        @block.sync
        def _(sp):
            for r in range(2):
                sp.sem_inc(stored[r], 16)
            with sp.Fori(0, 2) as i:
                def load(g):
                    h, j, r = g // 8, g % 8, g % 2
                    tok = slice(j * 2 * P, (j + 1) * 2 * P)
                    head = 2 * i + h
                    for half in range(2):
                        rows = slice(half * HD, (half + 1) * HD)
                        for dst, first in ((raw_k, G0["k"]), (raw_q, G0["q"])):
                            sp.dma_start(dst[r][rows], proj[first + head].rearrange("(m p) t -> p m t", m=2)[:, :, tok]
                                         ).then_inc(raw_loaded[r], 16)
                    sp.dma_start(raw_v[r][:], proj[G0["v"] + head, :, tok]).then_inc(raw_loaded[r], 16)

                def store(g):
                    h, j = g // 8, g % 8
                    sp.wait_ge(staged, STEPS * i + g + 1)
                    sp.sem_inc(sp_passed, 1)
                    sp.dma_start(o_out[2 * i + h, :, j * 2 * P:(j + 1) * 2 * P], o_stage[g % 2][:]
                                 ).then_inc(stored[g % 2], 16)

                load(0)
                load(1)
                for g in range(2, STEPS + 5):
                    if g < STEPS:
                        sp.wait_ge(split_lo, STEPS * i + g - 1)
                        sp.sem_inc(sp_passed, 1)
                        sp.wait_ge(turned, turns * i + turn_of["v", g - 2] + 1)
                        sp.sem_inc(sp_passed, 1)
                        load(g)
                    if g >= 5:
                        store(g - 5)
            for r in range(2):
                sp.wait_ge(stored[r], 16 * (STEPS + 1))

        @block.gpsimd
        def _(pool):
            with pool.Fori(0, 2) as i:
                def split(g):
                    h, j, r = g // 8, g % 8, g % 2
                    tok = slice(j * 2 * P, (j + 1) * 2 * P)
                    pool.wait_ge(split_hi, STEPS * i + g + 1)
                    pool.tensor_tensor(q_lo[r][:], raw_q[r][:], q_hi[r][:].bitcast(F32), ALU.subtract)
                    pool.tensor_tensor(k_stack[h][:, :, tok], raw_k[r][:], k_take[r][:], ALU.subtract
                                       ).then_inc(split_lo, 1)

                split(0)
                for u in range(UNITS + 1):
                    if u % 2 == 0 and u // 2 + 1 < STEPS:
                        split(u // 2 + 1)
                    if u >= 1:
                        v = u - 1
                        pool.wait_ge(weighted, UNITS * i + v + 1)
                        pool.sem_inc(pool_passed, 1)
                        for n, (at, keys) in enumerate(chunks(v)):
                            first, other = probs[v % 3][:, 0, at:at + keys], probs[v % 3][:, 1, at:at + keys]
                            scaled = pool.tensor_scalar(other, other, weight[v % 2][:, 1, n:n + 1], 1.0, ALU.mult, ALU.mult)
                            if (v, n) in by_vector:
                                scaled.then_inc(second, 1)
                            else:
                                pool.tensor_scalar(first, first, weight[v % 2][:, 0, n:n + 1], 1.0, ALU.mult, ALU.mult
                                                   ).then_inc(both_scaled, 1)
                                k = by_pool.index((v, n))
                                pool.wait_ge(both_scaled, len(by_pool) * i + k + 1)
                                pool.tensor_tensor(first, first, other, ALU.add).then_inc(pool_joined, 1)

        @block.scalar
        def _(act):
            act.preload_act_table_set("natural_log_exp_and_others")
            with act.Fori(0, 2) as i:
                def split(g):
                    h, j, r = g // 8, g % 8, g % 2
                    tok = slice(j * 2 * P, (j + 1) * 2 * P)
                    act.wait_ge(raw_loaded[r], LOADS * (STEPS // 2) * i + LOADS * (g // 2 + 1))
                    if g >= 2:
                        act.wait_ge(scores, 2 * CHUNKS * i + 2 * chunk_base[2 * g - 2])
                    act.activation(q_hi[r][:], raw_q[r][:], ACT.Copy)
                    act.activation(k_take[r][:].bitcast(F32R), raw_k[r][:], ACT.Copy, scale=c.lower[:]).then_inc(split_hi, 1)

                def values_hi(g):
                    t = turn_of["v", g]
                    act.wait_ge(turned, turns * i + t + 1)
                    act.activation(v_hi[g // 8][:, 2 * (g % 8):2 * (g % 8) + 2, :],
                                   t_bank[t % 2][:, 0:2 * P].rearrange("p (k n) -> p k n", n=P), ACT.Copy
                                   ).then_inc(turned_hi, 1)

                def factors(u):
                    if len(chunks(u)) > 1:
                        act.wait_ge(shifted, len(long_units) * i + long_units.index(u) + 1)
                        act.activation(factor[u % 2][:, :, 0:len(chunks(u))], shift[u % 2][:, :, 0:len(chunks(u))],
                                       ACT.Exp).then_inc(factored, 1)

                def exponentials(u, n):
                    at, keys = chunks(u)[n]
                    for m in range(2):
                        s = 2 * (chunk_base[u] + n) + m
                        if n == 0 and m == 0 and u >= 3:
                            last = len(chunks(u - 3)) - 1
                            act.wait_ge(turned, turns * i + turn_of[u - 3, last] + 1)
                        act.wait_ge(maxed, 2 * CHUNKS * i + s + 1)
                        act.activation(probs[u % 3][:, m, at:at + keys], s_bank[s % 4][:, 0:keys], ACT.Exp,
                                       bias=neg_max[u % 2][:, m, n:n + 1], accum_out=sums[u % 2][:, m, n:n + 1]
                                       ).then_inc(exped, 1)

                def weights_hi(u, n):
                    at, keys = chunks(u)[n]
                    t = turn_of[u, n]
                    if n == 0 and u % 2 == 0 and u >= 4:
                        act.wait_ge(output, STEPS * i + u // 2 - 1)
                    act.wait_ge(turned, turns * i + t + 1)
                    act.activation(wt_hi[u // 2 % 2][:, at // P:(at + keys) // P, (u % 2) * P:(u % 2 + 1) * P],
                                   t_bank[t % 2][:, 0:keys].rearrange("p (k n) -> p k n", n=P), ACT.Copy
                                   ).then_inc(turned_hi, 1)

                def take_output(g):
                    act.wait_ge(output, STEPS * i + g + 1)
                    act.wait_ge(stored[g % 2], 16 * (STEPS // 2) * i + 16 * (g // 2 + 1))
                    act.activation(o_stage[g % 2][:], o_bank[g % 2][:, 0:2 * P], ACT.Copy).then_inc(staged, 1)

                split(0)
                values_hi(0)
                split(1)
                for u in range(UNITS + 2):
                    for n in range(4):
                        if u >= 2 and n < len(chunks(u - 2)):
                            weights_hi(u - 2, n)
                        if 1 <= u <= UNITS and n == 0:
                            factors(u - 1)
                        if u < UNITS and n < len(chunks(u)):
                            exponentials(u, n)
                        if u % 2 == 0 and u >= 6 and n == 0:
                            take_output((u - 6) // 2)
                    if u % 2 == 1 and u // 2 + 2 < STEPS:
                        split(u // 2 + 2)
                    if u % 2 == 1 and u // 2 + 1 < STEPS:
                        values_hi(u // 2 + 1)
                take_output(STEPS - 2)
                take_output(STEPS - 1)

        @block.vector
        def _(dve):
            with dve.Fori(0, 2) as i:
                def values_lo(g):
                    t = turn_of["v", g]
                    tiles = slice(2 * (g % 8), 2 * (g % 8) + 2)
                    dve.wait_ge(turned_hi, turns * i + t + 1)
                    dve.tensor_tensor(v_lo[g // 8][:, tiles, :], t_bank[t % 2][:, 0:2 * P].rearrange("p (k n) -> p k n", n=P),
                                      v_hi[g // 8][:, tiles, :].bitcast(F32), ALU.subtract).then_inc(turned_lo, 1)

                def chain(ins, u, n):
                    ins.then_inc(stat, 1)
                    dve.wait_ge(stat, STATS * i + stat_base[u] + n)

                def weights(u):
                    r, k = u % 2, len(chunks(u))
                    dve.wait_ge(exped, 2 * CHUNKS * i + 2 * chunk_base[u + 1])
                    if k > 1:
                        dve.wait_ge(factored, len(long_units) * i + long_units.index(u) + 1)
                        for m in range(2):
                            both = dve.tensor_tensor_reduce(out=part[r][:, m, 0:k], in0=factor[r][:, m, 0:k],
                                                            in1=sums[r][:, m, 0:k], scale=1.0, scalar=0.0, op0=ALU.mult,
                                                            op1=ALU.add, accum_out=total[r][:, m:m + 1])
                        both.then_inc(stat, 1)
                    yield
                    if k > 1:
                        dve.wait_ge(stat, STATS * i + stat_base[u] + 2)
                        dve.reciprocal(inverse[r][:], total[r][:]).then_inc(stat, 1)
                    else:
                        dve.reciprocal(inverse[r][:], sums[r][:, :, 0]).then_inc(stat, 1)
                    yield
                    dve.wait_ge(stat, STATS * i + stat_base[u] + (3 if k > 1 else 1))
                    if k > 1:
                        for m in range(2):
                            w = dve.tensor_scalar(weight[r][:, m, 0:k], factor[r][:, m, 0:k], inverse[r][:, m:m + 1],
                                                  c.lam[:, m:m + 1], ALU.mult, ALU.mult)
                    else:
                        w = dve.tensor_tensor(weight[r][:, :, 0], inverse[r][:], c.lam[:], ALU.mult)
                    w.then_inc(weighted, 1)
                    yield

                def maxima(u, n):
                    at, keys = chunks(u)[n]
                    for m in range(2):
                        s = 2 * (chunk_base[u] + n) + m
                        dve.wait_ge(scores, 2 * CHUNKS * i + s + 1)
                        dve.tensor_reduce(neg_max[u % 2][:, m, n:n + 1], s_bank[s % 4][:, 0:keys], AX.X, ALU.max,
                                          negate=True).then_inc(maxed, 1)

                def shifts(u):
                    r, k = u % 2, len(chunks(u))
                    if k > 1:
                        dve.wait_ge(maxed, 2 * CHUNKS * i + 2 * chunk_base[u + 1])
                        chain(dve.tensor_reduce(least[r][:], neg_max[r][:, :, 0:k], AX.X, ALU.min), u, 1)
                        dve.tensor_tensor(shift[r][:, :, 0:k], least[r][:].unsqueeze(2).to_broadcast([P, 2, k]),
                                          neg_max[r][:, :, 0:k], ALU.subtract).then_inc(shifted, 1)

                def join(u, n):
                    at, keys = chunks(u)[n]
                    k = by_vector.index((u, n))
                    dve.wait_ge(second, len(by_vector) * i + k + 1)
                    first, other = probs[u % 3][:, 0, at:at + keys], probs[u % 3][:, 1, at:at + keys]
                    dve.scalar_tensor_tensor(first, first, weight[u % 2][:, 0, n:n + 1], other, ALU.mult, ALU.add
                                             ).then_inc(joined, 1)

                def weights_lo(u, n):
                    at, keys = chunks(u)[n]
                    t = turn_of[u, n]
                    where = (slice(None), slice(at // P, (at + keys) // P), slice((u % 2) * P, (u % 2 + 1) * P))
                    dve.wait_ge(turned_hi, turns * i + t + 1)
                    dve.tensor_tensor(wt_lo[u // 2 % 2][where], t_bank[t % 2][:, 0:keys].rearrange("p (k n) -> p k n", n=P),
                                      wt_hi[u // 2 % 2][where].bitcast(F32), ALU.subtract).then_inc(turned_lo, 1)

                values_lo(0)
                for u in range(UNITS + 2):
                    steps = weights(u - 1) if 1 <= u <= UNITS else iter(())
                    if u < UNITS:
                        maxima(u, 0)
                    next(steps, None)
                    if u >= 2:
                        weights_lo(u - 2, 0)
                    next(steps, None)
                    for n in range(4):
                        if n == 1:
                            next(steps, None)
                            if (u - 2, 3) in by_vector:
                                join(u - 2, 3)
                        if n > 0 and u < UNITS and n < len(chunks(u)):
                            maxima(u, n)
                        if n > 0 and u >= 2 and n < len(chunks(u - 2)):
                            weights_lo(u - 2, n)
                        if n > 0 and (u - 1, n - 1) in by_vector:
                            join(u - 1, n - 1)
                    if u < UNITS:
                        shifts(u)
                    if u % 2 == 1 and u // 2 + 1 < STEPS:
                        values_lo(u // 2 + 1)

        @block.tensor
        def _(pe):
            with pe.Fori(0, 2) as i:
                def turn_bank(t):
                    if t >= 2:
                        pe.wait_ge(turned_lo, turns * i + t - 1)

                def turn_values(g):
                    t = turn_of["v", g]
                    pe.wait_ge(raw_loaded[g % 2], LOADS * (STEPS // 2) * i + LOADS * (g // 2 + 1))
                    turn_bank(t)
                    for k in range(2):
                        tr = pe.transpose(t_bank[t % 2][:, k * P:(k + 1) * P], raw_v[g % 2][:, k * P:(k + 1) * P], c.ident[:])
                    tr.then_inc(turned, 1)

                def score(u, n):
                    h, g = u // TT, u // 2
                    at, keys = chunks(u)[n]
                    queries = slice((u % 2) * P, (u % 2 + 1) * P)
                    if n == 0 and u % 2 == 0:
                        pe.wait_ge(split_lo, STEPS * i + g + 1)
                    for m in range(2):
                        s = 2 * (chunk_base[u] + n) + m
                        if s >= 4:
                            pe.wait_ge(exped, 2 * CHUNKS * i + s - 3)
                        bank = s_bank[s % 4]
                        keys_moving = k_stack[h][:, m, at:at + keys]
                        pe.matmul(bank[:, 0:keys], q_hi[g % 2][:, m, queries], keys_moving, start=True, stop=False)
                        if at + keys == (u % TT + 1) * P:
                            pe.matmul(bank[:, keys - HD:keys], c.mask_q[:], c.mask_k[:], start=False, stop=False)
                        pe.matmul(bank[:, 0:keys], q_lo[g % 2][:, m, queries], keys_moving, start=False, stop=True
                                  ).then_inc(scores, 1)

                def turn_weights(u, n):
                    at, keys = chunks(u)[n]
                    t = turn_of[u, n]
                    if (u, n) in by_vector:
                        pe.wait_ge(joined, len(by_vector) * i + by_vector.index((u, n)) + 1)
                    else:
                        pe.wait_ge(pool_joined, len(by_pool) * i + by_pool.index((u, n)) + 1)
                    turn_bank(t)
                    for k in range(keys // P):
                        tr = pe.transpose(t_bank[t % 2][:, k * P:(k + 1) * P],
                                          probs[u % 3][:, 0, at + k * P:at + (k + 1) * P], c.ident[:])
                    tr.then_inc(turned, 1)

                def values(g, part, parts):
                    h, j, r = g // 8, g % 8, g % 2
                    if part == 0:
                        if g >= 2:
                            pe.wait_ge(staged, STEPS * i + g - 1)
                        last = turn_of[2 * g + 1, len(chunks(2 * g + 1)) - 1]
                        pe.wait_ge(turned_lo, turns * i + last + 1)
                    tiles = 2 * j + 2
                    for k in range(part * tiles // parts, (part + 1) * tiles // parts):
                        q = slice(P if k == tiles - 1 else 0, 2 * P)
                        out = o_bank[r][:, q]
                        pe.matmul(out, v_hi[h][:, k], wt_hi[r][:, k, q], start=(k == 0), stop=False)
                        pe.matmul(out, v_hi[h][:, k], wt_lo[r][:, k, q], start=False, stop=False)
                        mm = pe.matmul(out, v_lo[h][:, k], wt_hi[r][:, k, q], start=False, stop=(k == tiles - 1))
                    if part == parts - 1:
                        mm.then_inc(output, 1)

                turn_values(0)
                score(0, 0)
                for u in range(UNITS + 2):
                    for n in range(4):
                        if u >= 2 and n < len(chunks(u - 2)):
                            turn_weights(u - 2, n)
                        if (u, n) in every and (u, n) != every[-1]:
                            score(*every[every.index((u, n)) + 1])
                        if u >= 4:
                            values((u - 4) // 2, 4 * (u % 2) + n, 8)
                    if u % 2 == 1 and u // 2 + 1 < STEPS:
                        turn_values(u // 2 + 1)
                values(STEPS - 1, 0, 1)


def pooling(nc, c, proj, w, edge, b_out, w_next, w_next_hi, w_next_lo):
    RAWS = 4
    AT_ONCE = KT // len(WINDOWS)
    PAD = 16
    NGR = len(WINDOWS)
    with ExitStack() as ctx:
        def sb(name, shape, dt=F32):
            return ctx.enter_context(nc.sbuf_tensor("pl_" + name, shape, dt))

        def sem(name):
            return c.semaphore(nc, ctx, ("pl_" + name))

        u = [sb(f"u{r}", [P, PAD + SEQ]) for r in range(2)]
        run = [sb(f"run{r}", [P, PAD + SEQ]) for r in range(2)]
        diff = [sb(f"diff{r}", [P, SEQ]) for r in range(2)]
        d_hi = [sb(f"d_hi{r}", [P, SEQ], F32R) for r in range(2)]
        d_lo = [sb(f"d_lo{r}", [P, SEQ], F32R) for r in range(2)]
        w_raw, w_hi, w_lo = sb("w_raw", [P, NGR, P]), sb("w_hi", [P, NGR, P], F32R), sb("w_lo", [P, NGR, P], F32R)
        edges = sb("edges", [P, NGR, 16])
        next_raw = [sb(f"next_raw{r}", [P, DM]) for r in range(RAWS)]
        stage = [sb(f"stage{r}", [P, SB]) for r in range(4)]
        cleared, consts = sem("cleared"), sem("consts")
        u_loaded = [sem(f"u_loaded{r}") for r in range(2)]
        chained, differed = sem("chained"), sem("differed")
        hi_ready, lo_ready = sem("hi_ready"), sem("lo_ready")
        last_lo_ready = sem("last_lo_ready")
        w_hi_ready, w_lo_ready = sem("w_hi_ready"), sem("w_lo_ready")
        product, staged = sem("product"), sem("staged")
        stored = [sem(f"stored{r}") for r in range(4)]
        next_loaded = [sem(f"next_loaded{r}") for r in range(RAWS)]
        next_hi_ready, next_lo_ready = sem("next_hi_ready"), sem("next_lo_ready")
        block = ctx.enter_context(nc.Block())

        @block.sync
        def _(sp):
            def load_next(k):
                if k >= RAWS:
                    sp.wait_ge(next_lo_ready, k - RAWS + 1)
                sp.dma_start(next_raw[k % RAWS][:], w_next[k * P:(k + 1) * P]).then_inc(next_loaded[k % RAWS], 16)

            for g in range(NGR):
                if g >= 2:
                    sp.wait_ge(differed, g - 1)
                sp.dma_start(u[g % 2][:, PAD:], proj[G0["u"] + g]).then_inc(u_loaded[g % 2], 16)
                if g == 0:
                    sp.dma_start(w_raw[:], w.rearrange("g c d -> c g d")).then_inc(consts, 16)
                    sp.dma_start(edges[:], edge).then_inc(consts, 16)
                for k in range(g * AT_ONCE, (g + 1) * AT_ONCE):
                    load_next(k)
            for g in range(NGR):
                for s in range(NSB):
                    sp.wait_ge(staged, NSB * g + s + 1)
                    sp.dma_start(b_out[g, :, s * SB:(s + 1) * SB], stage[s][:]).then_inc(stored[s], 16)
            for s in range(NSB):
                sp.wait_ge(stored[s], 16 * NGR)

        @block.gpsimd
        def _(pool):
            for r in range(2):
                pool.memset(u[r][:, 0:PAD], 0.0)
                pool.memset(run[r][:, 0:PAD], 0.0).then_inc(cleared, 1)
            pool.wait_ge(w_hi_ready, 1)
            pool.tensor_tensor(w_lo[:], w_raw[:], w_hi[:].bitcast(F32), ALU.subtract).then_inc(w_lo_ready, 1)
            for g in range(NGR):
                for k in range(g * AT_ONCE, (g + 1) * AT_ONCE):
                    pool.wait_ge(next_hi_ready, k + 1)
                    pool.tensor_tensor(w_next_lo[:, k], next_raw[k % RAWS][:], w_next_hi[:, k].bitcast(F32), ALU.subtract
                                       ).then_inc(next_lo_ready, 1)
                if g < NGR - 1:
                    pool.wait_ge(hi_ready, g + 1)
                    pool.tensor_tensor(d_lo[g % 2][:], diff[g % 2][:], d_hi[g % 2][:].bitcast(F32), ALU.subtract
                                       ).then_inc(lo_ready, 1)

        @block.vector
        def _(dve):
            steps = 0

            def chain(ins):
                nonlocal steps
                steps += 1
                ins.then_inc(chained, 1)
                dve.wait_ge(chained, steps)

            dve.wait_ge(cleared, 2)
            for g, win in enumerate(WINDOWS):
                token = u[g % 2]
                dve.wait_ge(u_loaded[g % 2], 16 * (g // 2 + 1))
                src, span = token, 1
                for r in range(win.bit_length() - 1):
                    dst = run[r % 2]
                    chain(dve.tensor_tensor(dst[:, PAD:], src[:, PAD:], src[:, PAD - span:PAD + SEQ - span], ALU.add))
                    src, span = dst, 2 * span
                if g >= 2:
                    dve.wait_ge(lo_ready, g - 1)
                chain(dve.scalar_tensor_tensor(diff[g % 2][:], src[:, PAD:], 1.0 / win, token[:, PAD:],
                                               ALU.mult, ALU.subtract))
                if g == 0:
                    dve.wait_ge(consts, 32)
                chain(dve.tensor_tensor(diff[g % 2][:, 0:16], src[:, PAD:PAD + 16], edges[:, g, :], ALU.mult))
                dve.tensor_tensor(diff[g % 2][:, 0:16], diff[g % 2][:, 0:16], token[:, PAD:PAD + 16], ALU.subtract
                                  ).then_inc(differed, 1)
            r = (NGR - 1) % 2
            for s in range(NSB):
                tok = slice(s * SB, (s + 1) * SB)
                dve.wait_ge(hi_ready, NGR + s)
                dve.tensor_tensor(d_lo[r][:, tok], diff[r][:, tok], d_hi[r][:, tok].bitcast(F32), ALU.subtract
                                  ).then_inc(last_lo_ready, 1)

        @block.scalar
        def _(act):
            act.wait_ge(consts, 32)
            act.activation(w_hi[:], w_raw[:], ACT.Copy).then_inc(w_hi_ready, 1)

            def take(g):
                for s in range(NSB):
                    act.wait_ge(product, NSB * g + s + 1)
                    if g >= 1:
                        act.wait_ge(stored[s], 16 * g)
                    act.activation(stage[s][:], c.bank[4 * (g % 2) + s][:], ACT.Copy, scale=c.pool_scale[:, g:g + 1]
                                   ).then_inc(staged, 1)

            for g in range(NGR):
                for k in range(g * AT_ONCE, (g + 1) * AT_ONCE):
                    act.wait_ge(next_loaded[k % RAWS], 16 * (k // RAWS + 1))
                    act.activation(w_next_hi[:, k], next_raw[k % RAWS][:], ACT.Copy).then_inc(next_hi_ready, 1)
                act.wait_ge(differed, g + 1)
                if g >= 2:
                    act.wait_ge(product, NSB * (g - 1))
                for tok in [slice(0, SEQ)] if g < NGR - 1 else [slice(s * SB, (s + 1) * SB) for s in range(NSB)]:
                    act.activation(d_hi[g % 2][:, tok], diff[g % 2][:, tok], ACT.Copy).then_inc(hi_ready, 1)
                if g >= 1:
                    take(g - 1)
            take(NGR - 1)

        @block.tensor
        def _(pe):
            pe.wait_ge(w_lo_ready, 1)
            for g in range(NGR):
                if g < NGR - 1:
                    pe.wait_ge(lo_ready, g + 1)
                for s in range(NSB):
                    if g == NGR - 1:
                        pe.wait_ge(last_lo_ready, s + 1)
                    if g >= 2:
                        pe.wait_ge(staged, NSB * (g - 2) + s + 1)
                    bank, tok = c.bank[4 * (g % 2) + s][:], slice(s * SB, (s + 1) * SB)
                    pe.matmul(bank, w_hi[:, g], d_hi[g % 2][:, tok], start=True, stop=False)
                    pe.matmul(bank, w_hi[:, g], d_lo[g % 2][:, tok], start=False, stop=False)
                    pe.matmul(bank, w_lo[:, g], d_hi[g % 2][:, tok], start=False, stop=True).then_inc(product, 1)


SD = 256
NSD = SEQ // SD


def output_projection(nc, c, name, w, y_in, x_in, gain_post, h_out, heads=None, gain_pre=None, hn_out=None, weights=None):
    w_rows = None if weights else w.rearrange("(k p) n -> k p n", p=P)
    x_tiles = x_in.rearrange("(t p) d -> t p d", p=P)
    h_tiles = h_out.rearrange("(t p) d -> t p d", p=P)
    HALF = KT // 2
    with ExitStack() as ctx:
        def sb(nm, shape, dt=F32):
            return ctx.enter_context(nc.sbuf_tensor(f"{name}_{nm}", shape, dt))

        def sem(nm):
            return c.semaphore(nc, ctx, (f"{name}_{nm}"))

        if weights:
            w_hi, w_lo = weights
        else:
            w_hi, w_lo = sb("w_hi", [P, KT, DM], F32R), sb("w_lo", [P, KT, DM], F32R)
            w_raw = sb("w_raw", [P, KT, DM])
        y = [sb(f"y{p}", [P, KT, SD]) for p in range(2)]
        y_hi = [sb(f"y_hi{p}", [P, KT, SD], F32R) for p in range(2)]
        y_lo = [sb(f"y_lo{p}", [P, KT, SD], F32R) for p in range(2)]
        g_post = sb("g_post", [P, DM])
        x = [sb(f"x{q}", [P, DM]) for q in range(2)]
        h = [sb(f"h{q}", [P, DM]) for q in range(2)]
        junk = sb("junk", [P, DM])
        ss = [sb(f"ss{q}", [P, 4]) for q in range(2)]
        ln = [sb(f"ln{q}", [P, 2]) for q in range(2)]
        rstd = [sb(f"rstd{q}", [P, 2]) for q in range(2)]
        if heads:
            gate = [sb(f"gate{p}", [P, KT, SD]) for p in range(2)]
            square, rms = sb("square", [P, HALF, SD]), sb("rms", [P, HALF, SD])
        if hn_out is not None:
            g_pre = sb("g_pre", [P, DM])
            xs = sb("xs", [P, DM])
            n_stage = sb("n_stage", [P, KT, SD])

        gains_loaded = sem("gains_loaded")
        w_loaded = [sem(f"w_loaded{k}") for k in range(0 if weights else KT)]
        w_hi_ready = sem("w_hi_ready")
        w_lo_ready = [sem("w_lo_even"), sem("w_lo_odd")]
        heads_loaded = [sem(f"heads_loaded{p}") for p in range(2)]
        y_loaded = [sem(f"y_loaded{p}") for p in range(2)]
        x_loaded = [sem(f"x_loaded{q}") for q in range(2)]
        squared, summed = sem("squared"), sem("summed")
        logged, rms_ready = sem("logged"), sem("rms_ready")
        normed, o_gated, b_gated = sem("normed"), sem("o_gated"), sem("b_gated")
        b_hi_ready, o_hi_ready = sem("b_hi_ready"), sem("o_hi_ready")
        b_lo_ready, o_lo_ready = sem("b_lo_ready"), sem("o_lo_ready")
        product = sem("product")
        sums, sum_ready, post_ln, post_ready = sem("sums"), sem("sum_ready"), sem("post_ln"), sem("post_ready")
        post_done = sem("post_done")
        h_ready = sem("h_ready")
        h_sum, pre_ln, pre_ready = sem("h_sum"), sem("pre_ln"), sem("pre_ready")
        xs_ready, turned, n_staged = sem("xs_ready"), sem("turned"), sem("n_staged")
        h_stored = [sem(f"h_stored{q}") for q in range(2)]
        n_stored = sem("n_stored")
        passed = sem("passed")
        block = ctx.enter_context(nc.Block())
        y_bank, t_bank, m_bank = c.bank[0:4], c.bank[4:6], c.bank[6:8]
        Y_LOADS = 16 * (2 if heads else 1)

        def walk(slot, drain):
            def run(i, eng_first, eng_last):
                for p in range(2):
                    for q in range(2):
                        back = 2 * p + q

                        def lacks(tiles_back=0, blocks_ahead=0):
                            return (eng_first and back < tiles_back) or (eng_last and p + blocks_ahead > 1)

                        slot(i, p, q, 4 * i + back, 2 * i + p, lacks)

            return run

        def passes(eng, slot, drain=None):
            run = walk(slot, drain)
            run(0, True, False)
            with eng.Fori(1, NSD // 2 - 1) as i:
                run(i, False, False)
            run(NSD // 2 - 1, False, True)
            if drain:
                drain()

        def flat(ap):
            return ap.rearrange("p f t -> p (f t)")

        o_rows, b_rows = slice(0, HALF), slice(HALF, KT)

        @block.sync
        def _(sp):
            if hn_out is not None:
                sp.sem_inc(n_stored, 16)
            for q in range(2):
                sp.sem_inc(h_stored[q], 16)

            def load_y(s, p):
                tok = bass.ds(s * SD, SD)
                if heads:
                    for dst, src, loaded in ((y[p][:, o_rows], heads[0], heads_loaded), (gate[p][:], y_in, y_loaded),
                                             (y[p][:, b_rows], heads[1], y_loaded)):
                        sp.dma_start(dst, src[:, :, tok].rearrange("f p t -> p f t")).then_inc(loaded[p], 16)
                else:
                    sp.dma_start(y[p][:], y_in[:, :, tok].rearrange("f p t -> p f t")).then_inc(y_loaded[p], 16)

            def load_x(t, q):
                sp.dma_start(x[q][:], x_tiles[t]).then_inc(x_loaded[q], 16)

            load_y(0, 0)
            if not weights:
                for k in range(KT):
                    sp.dma_start(w_raw[:, k], w_rows[k]).then_inc(w_loaded[k], 16)
            sp.dma_start(g_post[:], bcast_row(gain_post, DM)).then_inc(gains_loaded, 16)
            if hn_out is not None:
                sp.dma_start(g_pre[:], bcast_row(gain_pre, DM)).then_inc(gains_loaded, 16)
            load_x(0, 0)
            load_y(1, 1)
            load_x(1, 1)

            def store_h(t, q):
                sp.wait_ge(h_ready, t + 1)
                sp.sem_inc(passed, 1)
                sp.dma_start(h_tiles[t], h[q][:]).then_inc(h_stored[q], 16)

            def store_n(s):
                sp.wait_ge(n_staged, 2 * s + 2)
                sp.sem_inc(passed, 1)
                sp.dma_start(hn_out[s], n_stage[:]).then_inc(n_stored, 16)

            def slot(i, p, q, t, s, lacks):
                if q == 0 and not lacks(blocks_ahead=2):
                    sp.wait_ge(o_lo_ready, s + 1)
                    sp.sem_inc(passed, 1)
                    sp.wait_ge(b_lo_ready, s + 1)
                    sp.sem_inc(passed, 1)
                    load_y(s + 2, p)
                if not lacks(tiles_back=1):
                    store_h(t - 1, 1 - q)
                    if not (lacks(blocks_ahead=1) and q == 1):
                        load_x(t + 1, 1 - q)
                if hn_out is not None and q == 1 and not lacks(tiles_back=3):
                    store_n(s - 1)

            def drain():
                store_h(TT - 1, 1)
                if hn_out is not None:
                    store_n(NSD - 1)
                    sp.wait_ge(n_stored, 16 * (NSD + 1))
                for q in range(2):
                    sp.wait_ge(h_stored[q], 16 * (TT // 2 + 1))

            passes(sp, slot, drain)

        @block.gpsimd
        def _(pool):
            def b_side(s, p, loads):
                if heads:
                    pool.wait_ge(y_loaded[p], Y_LOADS * loads)
                    pool.tensor_tensor(y[p][:, b_rows], y[p][:, b_rows], gate[p][:, b_rows], ALU.mult
                                       ).then_inc(b_gated, 1)

            def o_side(s, p):
                if heads:
                    pool.wait_ge(normed, s + 1)
                    pool.tensor_tensor(y[p][:, o_rows], y[p][:, o_rows], gate[p][:, o_rows], ALU.mult
                                       ).then_inc(o_gated, 1)
                pool.wait_ge(b_hi_ready, s + 1)
                pool.tensor_tensor(y_lo[p][:, b_rows], y[p][:, b_rows], y_hi[p][:, b_rows].bitcast(F32), ALU.subtract
                                   ).then_inc(b_lo_ready, 1)

            def residual(t, q, loads):
                pool.wait_ge(x_loaded[q], 16 * loads)
                pool.wait_ge(post_done, t + 1)
                pool.tensor_tensor(h[q][:], h[q][:], x[q][:], ALU.add).then_inc(h_ready, 1)

            b_side(0, 0, 1)
            o_side(0, 0)
            for k in range(0, 0 if weights else KT, 2):
                pool.wait_ge(w_hi_ready, k + 1)
                pool.tensor_tensor(w_lo[:, k], w_raw[:, k], w_hi[:, k].bitcast(F32), ALU.subtract
                                   ).then_inc(w_lo_ready[0], 1)

            def slot(i, p, q, t, s, lacks):
                if not lacks(tiles_back=1):
                    residual(t - 1, 1 - q, 2 * i + p + (1 if q == 1 else 0))
                if not lacks(blocks_ahead=1):
                    if q == 0:
                        b_side(s + 1, 1 - p, i + 1 + p)
                    else:
                        o_side(s + 1, 1 - p)

            passes(pool, slot, lambda: residual(TT - 1, 1, TT // 2))

        @block.scalar
        def _(act):
            act.preload_act_table_set("natural_log_exp_and_others")
            def squares(s, p, loads):
                if heads:
                    act.wait_ge(heads_loaded[p], 16 * loads)
                    act.activation(square[:], y[p][:, o_rows], ACT.Square).then_inc(squared, 1)

            def rms_of_heads(s):
                if heads:
                    for m in range(2):
                        act.wait_ge(summed, 2 * s + m + 1)
                        act.activation(flat(rms[:])[:, m * SB:(m + 1) * SB], m_bank[m][:], ACT.Ln, bias=c.eps[:],
                                       scale=1.0 / P).then_inc(logged, 1)
                    act.wait_ge(logged, 2 * s + 2)
                    act.activation(rms[:], rms[:], ACT.Exp, scale=-0.5).then_inc(rms_ready, 1)

            def his(s, p, loads):
                if heads:
                    act.wait_ge(b_gated, s + 1)
                else:
                    act.wait_ge(y_loaded[p], Y_LOADS * loads)
                act.activation(y_hi[p][:, b_rows], y[p][:, b_rows], ACT.Copy).then_inc(b_hi_ready, 1)
                if heads:
                    act.wait_ge(o_gated, s + 1)
                act.activation(y_hi[p][:, o_rows], y[p][:, o_rows], ACT.Copy).then_inc(o_hi_ready, 1)

            def post(t, q):
                act.wait_ge(product, t + 1)
                for m in range(2):
                    act.activation(junk[:, m * SB:(m + 1) * SB], y_bank[2 * q + m][:], ACT.Square,
                                   accum_out=ss[q][:, m:m + 1]).then_inc(sums, 1)
                act.wait_ge(sum_ready, t + 1)
                act.activation(ln[q][:, 0:1], ss[q][:, 2:3], ACT.Ln, bias=c.eps[:], scale=1.0 / DM).then_inc(post_ln, 1)
                act.wait_ge(post_ln, t + 1)
                act.activation(rstd[q][:, 0:1], ln[q][:, 0:1], ACT.Exp, scale=-0.5).then_inc(post_ready, 1)

            def pre(t, q):
                if hn_out is not None:
                    act.wait_ge(h_ready, t + 1)
                    act.activation(junk[:], h[q][:], ACT.Square, accum_out=ss[q][:, 3:4]).then_inc(h_sum, 1)
                    act.wait_ge(h_sum, t + 1)
                    act.activation(ln[q][:, 1:2], ss[q][:, 3:4], ACT.Ln, bias=c.eps[:], scale=1.0 / DM).then_inc(pre_ln, 1)
                    act.wait_ge(pre_ln, t + 1)
                    act.activation(rstd[q][:, 1:2], ln[q][:, 1:2], ACT.Exp, scale=-0.5).then_inc(pre_ready, 1)

            def stage_norm(t, q, s):
                if hn_out is not None:
                    if q == 0:
                        act.wait_ge(n_stored, 16 * (s + 1))
                    act.wait_ge(turned, t + 1)
                    for m in range(2):
                        n = act.activation(n_stage[:, 4 * m:4 * m + 4, q * P:(q + 1) * P],
                                           t_bank[m][:].rearrange("p (k n) -> p k n", k=4), ACT.Copy)
                    n.then_inc(n_staged, 1)

            squares(0, 0, 1)
            rms_of_heads(0)
            his(0, 0, 1)
            for k in range(0 if weights else KT):
                act.wait_ge(w_loaded[k], 16)
                act.activation(w_hi[:, k], w_raw[:, k], ACT.Copy).then_inc(w_hi_ready, 1)

            def slot(i, p, q, t, s, lacks):
                if not lacks(tiles_back=1):
                    post(t - 1, 1 - q)
                if not lacks(blocks_ahead=1):
                    if q == 0:
                        squares(s + 1, 1 - p, i + 1 + p)
                    else:
                        rms_of_heads(s + 1)
                if not lacks(tiles_back=2):
                    stage_norm(t - 2, q, s - 1)
                if not lacks(tiles_back=1):
                    pre(t - 1, 1 - q)
                if not lacks(blocks_ahead=1) and q == 1:
                    his(s + 1, 1 - p, i + 1 + p)

            def drain():
                post(TT - 1, 1)
                stage_norm(TT - 2, 0, NSD - 1)
                pre(TT - 1, 1)
                stage_norm(TT - 1, 1, NSD - 1)

            passes(act, slot, drain)

        @block.vector
        def _(dve):
            def subln(s, p):
                if heads:
                    dve.wait_ge(rms_ready, s + 1)
                    dve.scalar_tensor_tensor(flat(y[p][:, o_rows]), flat(y[p][:, o_rows]), c.subln[:], flat(rms[:]),
                                             ALU.mult, ALU.mult).then_inc(normed, 1)

            def o_lo(s, p):
                dve.wait_ge(o_hi_ready, s + 1)
                dve.tensor_tensor(y_lo[p][:, o_rows], y[p][:, o_rows], y_hi[p][:, o_rows].bitcast(F32), ALU.subtract
                                  ).then_inc(o_lo_ready, 1)

            def post(t, q, stores):
                dve.wait_ge(sums, 2 * t + 2)
                dve.tensor_tensor(ss[q][:, 2:3], ss[q][:, 0:1], ss[q][:, 1:2], ALU.add).then_inc(sum_ready, 1)
                dve.wait_ge(h_stored[q], 16 * stores)
                dve.wait_ge(post_ready, t + 1)
                for m in range(2):
                    cols = slice(m * SB, (m + 1) * SB)
                    z = dve.scalar_tensor_tensor(h[q][:, cols], y_bank[2 * q + m][:], rstd[q][:, 0:1], g_post[:, cols],
                                                 ALU.mult, ALU.mult)
                z.then_inc(post_done, 1)

            def pre(t, q):
                if hn_out is not None:
                    dve.wait_ge(pre_ready, t + 1)
                    dve.scalar_tensor_tensor(xs[:], h[q][:], rstd[q][:, 1:2], g_pre[:], ALU.mult, ALU.mult
                                             ).then_inc(xs_ready, 1)

            subln(0, 0)
            o_lo(0, 0)
            for k in range(1, 0 if weights else KT, 2):
                dve.wait_ge(w_hi_ready, k + 1)
                dve.tensor_tensor(w_lo[:, k], w_raw[:, k], w_hi[:, k].bitcast(F32), ALU.subtract
                                  ).then_inc(w_lo_ready[1], 1)
            dve.wait_ge(gains_loaded, 32 if hn_out is not None else 16)

            def slot(i, p, q, t, s, lacks):
                if not lacks(tiles_back=1):
                    post(t - 1, 1 - q, 2 * i + p + (1 if q == 1 else 0))
                if not lacks(blocks_ahead=1) and q == 1:
                    subln(s + 1, 1 - p)
                if not lacks(tiles_back=1):
                    pre(t - 1, 1 - q)
                if not lacks(blocks_ahead=1) and q == 1:
                    o_lo(s + 1, 1 - p)

            def drain():
                post(TT - 1, 1, TT // 2)
                pre(TT - 1, 1)

            passes(dve, slot, drain)

        @block.tensor
        def _(pe):
            def head_sums(s, ):
                if heads:
                    if not isinstance(s, int) or s > 0:
                        pe.wait_ge(logged, 2 * s)
                    pe.wait_ge(squared, s + 1)
                    for m in range(2):
                        pe.matmul(m_bank[m][:], c.ones[:], flat(square[:])[:, m * SB:(m + 1) * SB],
                                  start=True, stop=True).then_inc(summed, 1)

            def multiply(t, p, q, m):
                bank = y_bank[2 * q + m][:]
                tok, cols = slice(q * P, (q + 1) * P), slice(m * SB, (m + 1) * SB)
                for k in range(KT):
                    if not weights and isinstance(t, int) and t == 0:
                        pe.wait_ge(w_lo_ready[k % 2], k // 2 + 1)
                    pe.matmul(bank, y_hi[p][:, k, tok], w_hi[:, k, cols], start=(k == 0), stop=False)
                    pe.matmul(bank, y_hi[p][:, k, tok], w_lo[:, k, cols], start=False, stop=False)
                    mm = pe.matmul(bank, y_lo[p][:, k, tok], w_hi[:, k, cols], start=False, stop=(k == KT - 1))
                if m == 1:
                    mm.then_inc(product, 1)

            def turn(t):
                if hn_out is not None:
                    if not isinstance(t, int) or t > 0:
                        pe.wait_ge(n_staged, t)
                    pe.wait_ge(xs_ready, t + 1)
                    for k in range(KT):
                        tr = pe.transpose(t_bank[k // 4][:, (k % 4) * P:(k % 4 + 1) * P], xs[:, k * P:(k + 1) * P],
                                          c.ident[:])
                    tr.then_inc(turned, 1)

            head_sums(0)

            def slot(i, p, q, t, s, lacks):
                if q == 0:
                    pe.wait_ge(o_lo_ready, s + 1)
                    pe.wait_ge(b_lo_ready, s + 1)
                if not lacks(tiles_back=2):
                    pe.wait_ge(post_done, t - 1)
                multiply(t, p, q, 0)
                if not lacks(tiles_back=2):
                    turn(t - 2)
                multiply(t, p, q, 1)
                if q == 0 and not lacks(blocks_ahead=1):
                    head_sums(s + 1)

            def drain():
                turn(TT - 2)
                turn(TT - 1)

            passes(pe, slot, drain)


def sliding_window_attention(nc, c, proj, y_out):
    BT = 256
    BLOCKS = SEQ // BT
    PER = 8
    BATCHES = BLOCKS * PER
    UN = 4
    HEADS1 = 16
    KEEP = HD + BT
    PIECES = PER
    PH = HEADS1 // PIECES
    K_SLOT, V_SLOT = 3, 5
    with ExitStack() as ctx:
        def sb(name, shape, dt=F32):
            return ctx.enter_context(nc.sbuf_tensor("sw_" + name, shape, dt))

        def sem(name):
            return c.semaphore(nc, ctx, ("sw_" + name))

        raw_q = [sb(f"raw_q{p}", [P, HEADS1, BT]) for p in range(2)]
        q_hi = [sb(f"q_hi{p}", [P, BT // HD, HEADS1, HD], F32R) for p in range(2)]
        q_lo = [sb(f"q_lo{p}", [P, BT // HD, HEADS1, HD], F32R) for p in range(2)]
        raw_k = [sb(f"raw_k{p}", [P, 2, KEEP]) for p in range(2)]
        k_take = sb("k_take", [P, 2, KEEP])
        k_stack = [sb(f"k_stack{p}", [P, 2, KEEP], F32R) for p in range(2)]
        raw_v = [sb(f"raw_v{p}", [P, KEEP]) for p in range(2)]
        v_hi = [sb(f"v_hi{p}", [P, 4, 2, 2, HD], F32R) for p in range(2)]
        v_lo = [sb(f"v_lo{p}", [P, 4, 2, 2, HD], F32R) for p in range(2)]
        gate = [sb(f"gate{p}", [P, KT, BT]) for p in range(2)]
        y = [sb(f"y{p}", [P, KT, BT]) for p in range(2)]
        probs = [sb(f"probs{r}", [P, UN, P]) for r in range(4)]
        wt_hi = [sb(f"wt_hi{r}", [P, UN * P], F32R) for r in range(2)]
        wt_lo = [sb(f"wt_lo{r}", [P, UN * P], F32R) for r in range(2)]
        neg_sink, sink = sb("neg_sink", [P, 2, UN]), sb("sink", [P, 2, UN])
        neg_max = [sb(f"neg_max{r}", [P, UN]) for r in range(4)]
        shift = [sb(f"shift{r}", [P, UN]) for r in range(4)]
        sums = [sb(f"sums{r}", [P, UN]) for r in range(4)]
        sink_exp = [sb(f"sink_exp{r}", [P, UN]) for r in range(4)]
        total = [sb(f"total{r}", [P, UN]) for r in range(4)]
        inverse = [sb(f"inverse{r}", [P, UN]) for r in range(4)]

        qkv_loaded = [sem(f"qkv_loaded{p}") for p in range(2)]
        gate_loaded = [sem(f"gate_loaded{p}") for p in range(2)]
        cleared, sinks_ready = sem("cleared"), sem("sinks_ready")
        q_hi_ready, q_lo_ready = sem("q_hi_ready"), sem("q_lo_ready")
        k_hi_ready, k_ready = sem("k_hi_ready"), sem("k_ready")
        v_turned, v_hi_ready, v_ready = sem("v_turned"), sem("v_hi_ready"), sem("v_ready")
        scores, maxed, floored, exped = sem("scores"), sem("maxed"), sem("floored"), sem("exped")
        totalled, inverted, weighted = sem("totalled"), sem("inverted"), sem("weighted")
        turned, turned_hi, turned_lo = sem("turned"), sem("turned_hi"), sem("turned_lo")
        product, gated = sem("product"), sem("gated")
        stored = [sem(f"stored{p}") for p in range(2)]
        passed, pool_passed = sem("passed"), sem("pool_passed")
        block = ctx.enter_context(nc.Block())
        s_bank, t_bank, o_bank, v_bank = c.bank[0:4], c.bank[4:6], c.bank[6], c.bank[7]
        QKV = 80

        def by_head(q, heads):
            return q[:, :, heads].rearrange("p c h t -> p h c t")

        def chunked(q, heads):
            return q[:, heads].rearrange("p h (c t) -> p h c t", t=HD)

        def passes(eng, slot, drain=None):
            def run(i, first, last):
                for p in range(2):
                    for j in range(PER):
                        def lacks(back=0, ahead=0):
                            return (first and PER * p + j < back) or (last and p + ahead > 1)

                        slot(i, p, j, 2 * PER * i + PER * p + j, lacks)

            run(0, True, False)
            with eng.Fori(1, BLOCKS // 2 - 1) as i:
                run(i, False, False)
            run(BLOCKS // 2 - 1, False, True)
            if drain:
                drain()

        def before(p, j, n):
            at = PER * p + j - n
            return (at // PER) % 2, at % PER

        @block.sync
        def _(sp):
            for p in range(2):
                sp.sem_inc(stored[p], 16)

            def load(B, p, first=False):
                skip = HD if first else 0
                tok = bass.ds(B * BT, BT)
                window = slice(0, BT) if first else bass.ds(B * BT - HD, KEEP)
                for half in range(2):
                    rows = slice(half * HD, (half + 1) * HD)
                    sp.dma_start(raw_q[p][rows], proj[0:KT].rearrange("g (m p) t -> p (g m) t", m=2)[:, :, tok]
                                 ).then_inc(qkv_loaded[p], 16)
                    sp.dma_start(raw_k[p][rows, :, skip:], proj[G1["k"]].rearrange("(m p) t -> p m t", m=2)[:, :, window]
                                 ).then_inc(qkv_loaded[p], 16)
                sp.dma_start(raw_v[p][:, skip:], proj[G1["v"]][:, window]).then_inc(qkv_loaded[p], 16)

            def load_gate(B, p):
                sp.dma_start(gate[p][:], proj[G1["gate"]:G1["gate"] + KT][:, :, bass.ds(B * BT, BT)]
                             .rearrange("g p t -> p g t")).then_inc(gate_loaded[p], 16)

            def store(B, p):
                sp.wait_ge(gated, PER * B + PER)
                sp.sem_inc(passed, 1)
                sp.dma_start(y_out[:, :, bass.ds(B * BT, BT)].rearrange("g p t -> p g t"), y[p][:]).then_inc(stored[p], 16)

            load(0, 0, first=True)
            load(1, 1)
            load_gate(0, 0)

            def slot(i, p, j, b, lacks):
                B = 2 * i + p
                if j == 0 and not lacks(ahead=2):
                    for ready, n in ((q_lo_ready, PIECES * (B + 1)), (k_ready, B + 1), (v_turned, B + 1)):
                        sp.wait_ge(ready, n)
                        sp.sem_inc(passed, 1)
                    load(B + 2, p)
                if j == 4 and not lacks(back=8):
                    store(B - 1, 1 - p)
                if j == 4 and not lacks(ahead=1):
                    load_gate(B + 1, 1 - p)

            def drain():
                store(BLOCKS - 1, 1)
                for p in range(2):
                    sp.wait_ge(stored[p], 16 * (BLOCKS // 2 + 1))

            passes(sp, slot, drain)

        @block.gpsimd
        def _(pool):
            pool.memset(raw_k[0][:, :, 0:HD], 0.0).then_inc(cleared, 1)
            pool.memset(raw_v[0][:, 0:HD], 0.0).then_inc(cleared, 1)

            def split_q(B, p, piece):
                heads = slice(PH * piece, PH * piece + PH)
                pool.wait_ge(q_hi_ready, PIECES * B + piece + 1)
                pool.tensor_tensor(by_head(q_lo[p], heads), chunked(raw_q[p], heads),
                                   by_head(q_hi[p], heads).bitcast(F32), ALU.subtract
                                   ).then_inc(q_lo_ready, 1)

            def split_k(B, p):
                pool.wait_ge(k_hi_ready, B + 1)
                pool.tensor_tensor(k_stack[p][:], raw_k[p][:], k_take[:], ALU.subtract).then_inc(k_ready, 1)

            def normalize(b, r):
                pool.wait_ge(inverted, b + 1)
                pool.tensor_tensor(probs[r][:], probs[r][:], inverse[r][:].unsqueeze(2).to_broadcast([P, UN, P]),
                                   ALU.mult).then_inc(weighted, 1)

            split_k(0, 0)
            for piece in range(PIECES):
                split_q(0, 0, piece)

            def slot(i, p, j, b, lacks):
                if not lacks(back=1):
                    normalize(b - 1, (j - 1) % 4)
                if not lacks(ahead=1):
                    split_q(2 * i + p + 1, 1 - p, j)
                    if j == K_SLOT:
                        split_k(2 * i + p + 1, 1 - p)

            passes(pool, slot, lambda: normalize(BATCHES - 1, 3))

        @block.scalar
        def _(act):
            def split_q(B, p, piece, loads):
                heads = slice(PH * piece, PH * piece + PH)
                act.wait_ge(qkv_loaded[p], QKV * loads)
                act.activation(by_head(q_hi[p], heads), chunked(raw_q[p], heads), ACT.Copy).then_inc(q_hi_ready, 1)

            def split_k(B, p):
                act.activation(k_take[:].bitcast(F32R), raw_k[p][:], ACT.Copy, scale=c.lower[:]).then_inc(k_hi_ready, 1)

            def values_hi(B, p):
                act.wait_ge(v_turned, B + 1)
                act.activation(v_hi[p][:], v_bank[:].rearrange("p (w k d) -> p w k d", w=4, k=2).unsqueeze(3)
                               .to_broadcast([P, 4, 2, 2, HD]), ACT.Copy).then_inc(v_hi_ready, 1)

            def exponentials(b, p, j):
                r = j % 4
                act.wait_ge(floored, b + 1)
                for u in range(UN):
                    act.activation(probs[r][:, u], s_bank[r][:, u * P:(u + 1) * P], ACT.Exp, bias=neg_max[r][:, u:u + 1],
                                   accum_out=sums[r][:, u:u + 1])
                act.activation(sink_exp[r][:], shift[r][:], ACT.Exp).then_inc(exped, 1)

            def weights_hi(b, r, lacks=None):
                if lacks is None or not lacks(back=5):
                    act.wait_ge(product, b - 1)
                act.wait_ge(turned, b + 1)
                act.activation(wt_hi[r][:], t_bank[r][:], ACT.Copy).then_inc(turned_hi, 1)

            act.preload_act_table_set("natural_log_exp_and_others")
            act.wait_ge(cleared, 2)
            act.wait_ge(qkv_loaded[0], QKV)
            split_k(0, 0)
            values_hi(0, 0)
            for piece in range(PIECES):
                split_q(0, 0, piece, 1)

            def slot(i, p, j, b, lacks):
                if not lacks(back=3):
                    weights_hi(b - 3, (j - 3) % 2, lacks)
                if not lacks(ahead=1):
                    B = 2 * i + p + 1
                    split_q(B, 1 - p, j, i + 1 + p)
                    if j == K_SLOT:
                        split_k(B, 1 - p)
                    if j == V_SLOT:
                        values_hi(B, 1 - p)
                exponentials(b, p, j)

            def drain():
                for b in range(BATCHES - 3, BATCHES):
                    weights_hi(b, b % 2)

            passes(act, slot, drain)

        @block.vector
        def _(dve):
            for half in range(2):
                rows = slice(half * HD, (half + 1) * HD)
                dve.tensor_copy(sink[rows], c.sinks[rows].rearrange("p (k u m) -> p k u m", k=2, m=2)[:, :, :, half])
                dve.tensor_scalar(neg_sink[rows], c.sinks[rows].rearrange("p (k u m) -> p k u m", k=2, m=2)[:, :, :, half],
                                  -1.0, None, ALU.mult).then_inc(sinks_ready, 1)
            dve.wait_ge(sinks_ready, 2)

            def values_lo(B, p):
                dve.wait_ge(v_hi_ready, B + 1)
                windows = v_bank[:].rearrange("p (w k d) -> p w k d", w=4, k=2)
                for twice in range(2):
                    lo = dve.tensor_tensor(v_lo[p][:, :, :, twice], windows, v_hi[p][:, :, :, twice].bitcast(F32),
                                           ALU.subtract)
                lo.then_inc(v_ready, 1)

            def maxima(b, j, lacks):
                r, kv, r1 = j % 4, j % 2, (j - 1) % 4
                dve.wait_ge(scores, b + 1)
                dve.tensor_reduce(neg_max[r][:], s_bank[r][:].rearrange("p (u k) -> p u k", u=UN), AX.X, ALU.max,
                                  negate=True).then_inc(maxed, 1)
                if not lacks(back=1):
                    totals(b - 1, r1)
                dve.wait_ge(maxed, 2 * b + 1)
                dve.tensor_tensor(neg_max[r][:], neg_max[r][:], neg_sink[:, kv], ALU.min).then_inc(maxed, 1)
                if not lacks(back=1):
                    inverses(b - 1, r1)
                dve.wait_ge(maxed, 2 * b + 2)
                dve.tensor_tensor(shift[r][:], sink[:, kv], neg_max[r][:], ALU.add).then_inc(floored, 1)

            def totals(b, r):
                dve.wait_ge(exped, b + 1)
                dve.tensor_tensor(total[r][:], sums[r][:], sink_exp[r][:], ALU.add).then_inc(totalled, 1)

            def inverses(b, r):
                dve.wait_ge(totalled, b + 1)
                dve.reciprocal(inverse[r][:], total[r][:]).then_inc(inverted, 1)

            def weights_lo(b, r):
                dve.wait_ge(turned_hi, b + 1)
                dve.tensor_tensor(wt_lo[r][:], t_bank[r][:], wt_hi[r][:].bitcast(F32), ALU.subtract).then_inc(turned_lo, 1)

            def take(b, p, j, B_loads, stores):
                kv, tok = j % 2, slice((j // 2) * HD, (j // 2 + 1) * HD)
                if j == 0:
                    dve.wait_ge(gate_loaded[p], 16 * B_loads)
                    dve.wait_ge(stored[p], 16 * B_loads)
                dve.wait_ge(product, b + 1)
                for half in range(2):
                    rows = slice(half * HD, (half + 1) * HD)
                    groups = slice(UN * kv, UN * kv + UN)
                    last = dve.tensor_tensor(y[p][rows, groups, tok],
                                             o_bank[rows].rearrange("p (u m q) -> p u m q", u=UN, m=2)[:, :, half],
                                             gate[p][rows, groups, tok], ALU.mult)
                last.then_inc(gated, 1)

            values_lo(0, 0)

            def slot(i, p, j, b, lacks):
                if not lacks(back=5):
                    pb, jb = before(p, j, 5)
                    loads = i + 1 if not (p == 0 and j < 5) else i
                    take(b - 5, pb, jb, loads, None)
                maxima(b, j, lacks)
                if not lacks(back=3):
                    weights_lo(b - 3, (j - 3) % 2)
                if not lacks(ahead=1) and j == V_SLOT:
                    values_lo(2 * i + p + 1, 1 - p)

            def drain():
                totals(BATCHES - 1, 3)
                inverses(BATCHES - 1, 3)
                for b in range(BATCHES, BATCHES + 5):
                    take(b - 5, 1, (b - 5) % PER, BLOCKS // 2, None)
                    if b - 3 < BATCHES:
                        weights_lo(b - 3, (b - 3) % 2)

            passes(dve, slot, drain)

        @block.tensor
        def _(pe):
            def turn_values(B, p, loads):
                if loads is not None:
                    pe.wait_ge(qkv_loaded[p], QKV * loads)
                if not isinstance(B, int) or B > 0:
                    pe.wait_ge(v_ready, B)
                for w in range(4):
                    tr = pe.transpose(v_bank[:, w * P:(w + 1) * P], raw_v[p][:, w * HD:w * HD + P], c.ident[:])
                tr.then_inc(v_turned, 1)

            def score(b, p, j, B, first, lacks):
                n, kv, r = j // 2, j % 2, j % 4
                if j < 2:
                    pe.wait_ge(q_lo_ready, PIECES * B + (j + 1) * PIECES // 2)
                if j == 0:
                    pe.wait_ge(k_ready, B + 1)
                if not lacks(back=4):
                    pe.wait_ge(exped, b - 3)
                keys = k_stack[p][:, kv, n * HD:n * HD + P]
                for u in range(UN):
                    bank = s_bank[r][:, u * P:(u + 1) * P]
                    heads = slice(8 * kv + 2 * u, 8 * kv + 2 * u + 2)
                    pe.matmul(bank, q_hi[p][:, n, heads], keys, start=True, stop=False)
                    if first:
                        pe.matmul(bank[:, 0:HD], c.mask_all[:], c.mask_k[:], start=False, stop=False)
                    mm = pe.matmul(bank, q_lo[p][:, n, heads], keys, start=False, stop=True)
                mm.then_inc(scores, 1)

            def turn_weights(b, j, lacks):
                if not lacks(back=4):
                    pe.wait_ge(turned_lo, b - 1)
                pe.wait_ge(weighted, b + 1)
                for u in range(UN):
                    tr = pe.transpose(t_bank[j % 2][:, u * P:(u + 1) * P], probs[j % 4][:, u], c.ident[:])
                tr.then_inc(turned, 1)

            def values(b, p, j, lacks):
                n, kv, r = j // 2, j % 2, j % 2
                if not lacks(back=5):
                    pe.wait_ge(gated, b)
                pe.wait_ge(turned_lo, b + 1)
                pe.matmul(o_bank[:], v_hi[p][:, n, kv], wt_hi[r][:], start=True, stop=False)
                pe.matmul(o_bank[:], v_hi[p][:, n, kv], wt_lo[r][:], start=False, stop=False)
                pe.matmul(o_bank[:], v_lo[p][:, n, kv], wt_hi[r][:], start=False, stop=True).then_inc(product, 1)

            pe.wait_ge(cleared, 2)
            turn_values(0, 0, 1)

            def slot(i, p, j, b, lacks):
                B = 2 * i + p
                if j == 0:
                    pe.wait_ge(v_ready, B + 1)
                if j == V_SLOT - 1 and not lacks(ahead=1):
                    turn_values(B + 1, 1 - p, i + 1 + p)
                score(b, p, j, B, isinstance(b, int) and b < 2, lacks)
                if not lacks(back=2):
                    turn_weights(b - 2, (j - 2) % PER, lacks)
                if not lacks(back=4):
                    pb, jb = before(p, j, 4)
                    values(b - 4, pb, jb, lacks)

            def drain():
                none = lambda back=0, ahead=0: False
                for b in range(BATCHES, BATCHES + 4):
                    if b - 2 < BATCHES:
                        turn_weights(b - 2, (b - 2) % PER, none)
                    values(b - 4, 1, (b - 4) % PER, none)

            passes(pe, slot, drain)


def build(nc, a, out):
    def dram(name, shape, dt=F32):
        return nc.dram_tensor(name, shape, dt).ap()

    proj0, proj1 = dram("proj0", (NG0, P, SEQ)), dram("proj1", (NG1, P, SEQ))
    heads0, pooled0 = dram("heads0", (4, P, SEQ)), dram("pooled0", (4, P, SEQ))
    h1 = dram("h1", (SEQ, DM))
    hn1 = dram("hn1", (NSD, P, KT, SD))
    y1 = dram("y1", (KT, P, SEQ))
    c = Core()
    c.rope_cos, c.rope_sin = a["rope_cos"], a["rope_sin"]
    with ExitStack() as ctx:
        def sb(name, shape, dt=F32):
            return ctx.enter_context(nc.sbuf_tensor(name, shape, dt))

        c.bank = [ctx.enter_context(nc.psum_tensor(f"bank{i}", [P, SB], F32)) for i in range(8)]
        c.ident, c.ones, c.eps = sb("ident", [P, P]), sb("ones", [P, P]), sb("eps", [P, 1])
        c.lam, c.subln, c.lower = sb("lam", [P, 2]), sb("subln", [P, 1]), sb("lower", [P, 1])
        c.pool_scale, c.sinks = sb("pool_scale", [P, len(WINDOWS)]), sb("sinks", [P, 16])
        c.mask_q, c.mask_all, c.mask_k = sb("mask_q", [P, P], F32R), sb("mask_all", [P, P], F32R), sb("mask_k", [P, HD], F32R)

        phase_constants(nc, c, a)
        with ExitStack() as layer:
            hn_hi = layer.enter_context(nc.sbuf_tensor("hn0_hi", [P, KT, SEQ], F32R))
            hn_lo = layer.enter_context(nc.sbuf_tensor("hn0_lo", [P, KT, SEQ], F32R))
            in_projection(nc, "in0", c, a["ab_w_in"][0], hn_hi, hn_lo, PARTS0, proj0,
                          norm=(a["x"][0], a["norm_pre"][0]))
        differential_attention(nc, c, proj0, heads0)
        with ExitStack() as layer:
            w_hi = layer.enter_context(nc.sbuf_tensor("w_out0_hi", [P, KT, DM], F32R))
            w_lo = layer.enter_context(nc.sbuf_tensor("w_out0_lo", [P, KT, DM], F32R))
            pooling(nc, c, proj0, a["pool_w"][0], a["pool_edge"], pooled0, a["ab_w_out"][0], w_hi, w_lo)
            output_projection(nc, c, "out0", None, proj0[G0["gate"]:G0["gate"] + KT], a["x"][0],
                              a["norm_post"][0], h1, heads=(heads0, pooled0), gain_pre=a["norm_pre"][1], hn_out=hn1,
                              weights=(w_hi, w_lo))
        c.clear_spent(nc)
        with ExitStack() as layer:
            hn_hi = layer.enter_context(nc.sbuf_tensor("hn1_hi", [P, KT, SEQ], F32R))
            hn_lo = layer.enter_context(nc.sbuf_tensor("hn1_lo", [P, KT, SEQ], F32R))
            in_projection(nc, "in1", c, a["c_w_in"][0], hn_hi, hn_lo, PARTS1, proj1, load=hn1)
        sliding_window_attention(nc, c, proj1, y1)
        output_projection(nc, c, "out1", a["c_w_out"][0], y1, h1, a["norm_post"][1], out[0])


_INS = ["x", "norm_pre", "norm_post", "ab_w_in", "ab_w_out", "diff_lambda", "diff_subln",
        "pool_w", "pool_scale", "c_w_in", "c_w_out", "c_sinks"]


def kernel(**inputs):
    import concourse.bacc as bacc
    from concourse.bass_utils import run_bass_kernel_spmd as run

    nc = bacc.Bacc("TRN2", target_bir_lowering=False, num_devices=1)
    arrays = {name: np.ascontiguousarray(inputs[name]) for name in _INS}
    arrays["rope_cos"], arrays["rope_sin"] = rope_tables()
    arrays["pool_edge"] = pool_edge()
    arrays = {f"in_{name}": array for name, array in arrays.items()}
    args = {name[3:]: nc.dram_tensor(name, array.shape, mybir.dt.from_np(array.dtype), kind="ExternalInput").ap()
            for name, array in arrays.items()}
    out = nc.dram_tensor("out_0", (1, SEQ, DM), F32, kind="ExternalOutput").ap()
    build(nc, args, out)
    result = run(nc, [arrays], core_ids=[0])
    return result.results[0]["out_0"]
```
